# Optimizing a Trainium2 kernel written in Bass

```python
import jax, jax.numpy as jnp
from jax import lax
import numpy as np

D_MODEL = 1024
BATCH = 1
SEQ = 128
DEPTH = 1
DEC_BATCH = 1
DEC_SEQ = 256
PAST_LEN = 128

GRID_W = 64
FOURIER_WIDTH = D_MODEL
N_FOURIER_GROUPS = 8
FOURIER_GROUP_DIM = FOURIER_WIDTH // N_FOURIER_GROUPS
N_RET_HEADS = D_MODEL // 256
RET_HEAD_DIM = 128
RET_WIDTH = N_RET_HEADS * RET_HEAD_DIM
CHUNK = 128
IN_WIDTH = FOURIER_WIDTH + 4 * RET_WIDTH + 2 * D_MODEL
N_EXPERTS = 64
N_EXPERT_GROUPS = 8
TOPK_GROUPS = 4
TOP_K = 8
EXPERT_DIM = 256
SHARED_DIM = 256
ROUTED_SCALE = 2.5
ROPE_BASE = 10000.0
EPS = 1e-6

kernel_name = 'hybrid_fnet_retention_moe_diffusion_step'

def _rmsnorm(x, g):
    xf = x.astype(jnp.float32)
    y = xf * lax.rsqrt(jnp.mean(xf * xf, axis=-1, keepdims=True) + EPS)
    return (y * g.astype(jnp.float32)).astype(x.dtype)

def _grid_rope(length):
    rows = length // GRID_W
    r = jnp.repeat(jnp.arange(rows, dtype=jnp.float32), GRID_W)
    col = jnp.tile(jnp.arange(GRID_W, dtype=jnp.float32), rows)
    nf = RET_HEAD_DIM // 4
    inv = ROPE_BASE ** (-jnp.arange(nf, dtype=jnp.float32) / nf)
    ar = r[:, None] * inv[None]
    ac = col[:, None] * inv[None]
    ang = jnp.concatenate([ar, ar, ac, ac], axis=-1)[:, None, :]
    return jnp.cos(ang), jnp.sin(ang)

def _apply_rope(x, cos, sin):
    nf = RET_HEAD_DIM // 4
    xs = x.reshape(*x.shape[:-1], 2, 2, nf)
    rot = jnp.stack([-xs[..., 1, :], xs[..., 0, :]], axis=-2).reshape(x.shape)
    return x * cos + rot * sin

def _retention_scan(q, k, v, log_gamma, s0, include_diag):
    b, length, h, dk = q.shape
    dv = v.shape[-1]
    n = length // CHUNK
    qc = q.reshape(b, n, CHUNK, h, dk)
    kc = k.reshape(b, n, CHUNK, h, dk)
    vc = v.reshape(b, n, CHUNK, h, dv)
    pos = jnp.arange(CHUNK, dtype=jnp.float32)
    diff = pos[:, None] - pos[None, :]
    allowed = (diff >= 0) if include_diag else (diff > 0)
    decay = jnp.where(allowed[None], jnp.exp(log_gamma[:, None, None] * jnp.where(allowed, diff, 0.0)[None]), 0.0)
    scores = jnp.einsum('bnihd,bnjhd->bnhij', qc, kc) * decay[None, None]
    intra = jnp.einsum('bnhij,bnjhe->bnihe', scores, vc)
    k_w = jnp.exp(log_gamma[:, None] * (CHUNK - 1.0 - pos)[None])
    kv = jnp.einsum('bnjhd,hj,bnjhe->nbhde', kc, k_w, vc)
    g_chunk = jnp.exp(log_gamma * CHUNK)[None, :, None, None]

    def step(s, kv_n):
        return g_chunk * s + kv_n, s

    s_final, s_prev = lax.scan(step, s0, kv)
    q_w = jnp.exp(log_gamma[:, None] * (pos + 1.0)[None])
    cross = jnp.einsum('bnihd,hi,nbhde->bnihe', qc, q_w, s_prev)
    return (intra + cross).reshape(b, length, h, dv), s_final

def _parallel_mixer(h, s0_f, s0_b, rope, w_in, decay_f, decay_b, gn_g, w_four, w_ret, w_o):
    b, length, _ = h.shape
    proj = h @ w_in
    cuts = [FOURIER_WIDTH, FOURIER_WIDTH + RET_WIDTH, FOURIER_WIDTH + 2 * RET_WIDTH,
            FOURIER_WIDTH + 3 * RET_WIDTH, FOURIER_WIDTH + 4 * RET_WIDTH,
            FOURIER_WIDTH + 4 * RET_WIDTH + D_MODEL]
    u_f, q, k, v, g, gate_f, gate_r = jnp.split(proj, cuts, axis=-1)
    uf = u_f.reshape(b, length, N_FOURIER_GROUPS, FOURIER_GROUP_DIM).astype(jnp.float32)
    f_mix = jnp.fft.fftn(uf, axes=(1, 3), norm='ortho').real
    f_out = f_mix.reshape(b, length, FOURIER_WIDTH).astype(h.dtype) @ w_four
    q = q.reshape(b, length, N_RET_HEADS, RET_HEAD_DIM).astype(jnp.float32)
    k = k.reshape(b, length, N_RET_HEADS, RET_HEAD_DIM).astype(jnp.float32)
    v = v.reshape(b, length, N_RET_HEADS, RET_HEAD_DIM).astype(jnp.float32)
    if rope is not None:
        cos, sin = rope
        q = _apply_rope(q, cos, sin)
        k = _apply_rope(k, cos, sin)
    q = q * (RET_HEAD_DIM ** -0.5)
    lg_f = jax.nn.log_sigmoid(decay_f.astype(jnp.float32))
    lg_b = jax.nn.log_sigmoid(decay_b.astype(jnp.float32))
    o_f, s_f = _retention_scan(q, k, v, lg_f, s0_f.astype(jnp.float32), True)
    o_b, s_b = _retention_scan(q[:, ::-1], k[:, ::-1], v[:, ::-1], lg_b, s0_b.astype(jnp.float32), False)
    o = o_f + o_b[:, ::-1]
    mu = jnp.mean(o, axis=-1, keepdims=True)
    var = jnp.mean(jnp.square(o - mu), axis=-1, keepdims=True)
    o = ((o - mu) * lax.rsqrt(var + EPS)).reshape(b, length, RET_WIDTH) * gn_g.astype(jnp.float32)
    r_out = (o.astype(h.dtype) * jax.nn.silu(g)) @ w_ret
    merged = jax.nn.sigmoid(gate_f) * f_out + jax.nn.sigmoid(gate_r) * r_out
    return merged @ w_o, s_f, s_b

def _moe(h, w_router, router_bias, we_g, we_u, we_d, ws_g, ws_u, ws_d):
    b, length, d = h.shape
    t = h.reshape(b * length, d)
    scores = jax.nn.sigmoid((t @ w_router).astype(jnp.float32))
    biased = scores + router_bias.astype(jnp.float32)
    per_group = N_EXPERTS // N_EXPERT_GROUPS
    grouped = biased.reshape(-1, N_EXPERT_GROUPS, per_group)
    group_score = jnp.sum(lax.top_k(grouped, 2)[0], axis=-1)
    _, g_idx = lax.top_k(group_score, TOPK_GROUPS)
    g_mask = jnp.sum(jax.nn.one_hot(g_idx, N_EXPERT_GROUPS, dtype=jnp.float32), axis=1) > 0
    e_mask = jnp.repeat(g_mask, per_group, axis=-1)
    _, idx = lax.top_k(jnp.where(e_mask, biased, -jnp.inf), TOP_K)
    w = jnp.take_along_axis(scores, idx, axis=-1)
    w = w / jnp.sum(w, axis=-1, keepdims=True) * ROUTED_SCALE
    combine = jnp.einsum('tk,tke->te', w, jax.nn.one_hot(idx, N_EXPERTS, dtype=jnp.float32)).astype(h.dtype)
    hid = jax.nn.silu(jnp.einsum('td,edf->tef', t, we_g)) * jnp.einsum('td,edf->tef', t, we_u)
    routed = jnp.einsum('tef,efd->td', hid * combine[..., None], we_d)
    shared = (jax.nn.silu(t @ ws_g) * (t @ ws_u)) @ ws_d
    return (routed + shared).reshape(b, length, d)

def _trunk_layer(x, cond, s0_f, s0_b, rope, w_ada, b_ada, norm1_g, norm2_g, w_in, decay_f, decay_b, gn_g,
                 w_four, w_ret, w_o, w_router, router_bias, we_g, we_u, we_d, ws_g, ws_u, ws_d):
    mod = jax.nn.silu(cond) @ w_ada + b_ada
    sh1, sc1, g1, sh2, sc2, g2 = jnp.split(mod[:, None, :], 6, axis=-1)
    h = _rmsnorm(x, norm1_g) * (1.0 + sc1) + sh1
    mix, s_f, s_b = _parallel_mixer(h, s0_f, s0_b, rope, w_in, decay_f, decay_b, gn_g, w_four, w_ret, w_o)
    x = x + g1 * mix
    h = _rmsnorm(x, norm2_g) * (1.0 + sc2) + sh2
    x = x + g2 * _moe(h, w_router, router_bias, we_g, we_u, we_d, ws_g, ws_u, ws_d)
    return x, s_f, s_b

def setup_inputs(seed: int = 0) -> dict:
    key = jax.random.key(seed)
    ks = jax.random.split(key, 32)
    f32 = jnp.float32
    n = lambda i, shape, s: jax.random.normal(ks[i], shape, f32) * s
    gam = 1.0 - 2.0 ** (-5.0 - jnp.arange(N_RET_HEADS, dtype=f32))
    decay0 = jnp.log(gam) - jnp.log1p(-gam)
    st_shape = (DEC_BATCH, DEPTH, N_RET_HEADS, RET_HEAD_DIM, RET_HEAD_DIM)
    return {
        'x_prompt': n(0, (BATCH, SEQ, D_MODEL), 1.0),
        'x_sample': n(1, (DEC_BATCH, DEC_SEQ, D_MODEL), 1.0),
        'state_ret_fwd': n(2, st_shape, 0.5),
        'state_ret_bwd': n(3, st_shape, 0.5),
        'c': n(4, (DEC_BATCH, D_MODEL), 1.0),
        'c_ctx': n(5, (D_MODEL,), 1.0),
        'w_ada': n(6, (DEPTH, D_MODEL, 6 * D_MODEL), 0.5 * D_MODEL ** -0.5),
        'b_ada': n(7, (DEPTH, 6 * D_MODEL), 0.02),
        'norm1_g': 1.0 + n(8, (DEPTH, D_MODEL), 0.01),
        'norm2_g': 1.0 + n(9, (DEPTH, D_MODEL), 0.01),
        'w_in': n(10, (DEPTH, D_MODEL, IN_WIDTH), D_MODEL ** -0.5),
        'ret_decay_fwd': decay0[None] + n(11, (DEPTH, N_RET_HEADS), 0.01),
        'ret_decay_bwd': decay0[None] + n(12, (DEPTH, N_RET_HEADS), 0.01),
        'ret_gn_g': 1.0 + n(13, (DEPTH, RET_WIDTH), 0.01),
        'w_four_out': n(14, (DEPTH, FOURIER_WIDTH, D_MODEL), FOURIER_WIDTH ** -0.5),
        'w_ret_out': n(15, (DEPTH, RET_WIDTH, D_MODEL), RET_WIDTH ** -0.5),
        'w_out': n(16, (DEPTH, D_MODEL, D_MODEL), D_MODEL ** -0.5),
        'w_router': n(17, (DEPTH, D_MODEL, N_EXPERTS), D_MODEL ** -0.5),
        'router_bias': n(18, (DEPTH, N_EXPERTS), 0.01),
        'w_exp_gate': n(19, (DEPTH, N_EXPERTS, D_MODEL, EXPERT_DIM), D_MODEL ** -0.5),
        'w_exp_up': n(20, (DEPTH, N_EXPERTS, D_MODEL, EXPERT_DIM), D_MODEL ** -0.5),
        'w_exp_down': n(21, (DEPTH, N_EXPERTS, EXPERT_DIM, D_MODEL), EXPERT_DIM ** -0.5),
        'w_shared_gate': n(22, (DEPTH, D_MODEL, SHARED_DIM), D_MODEL ** -0.5),
        'w_shared_up': n(23, (DEPTH, D_MODEL, SHARED_DIM), D_MODEL ** -0.5),
        'w_shared_down': n(24, (DEPTH, SHARED_DIM, D_MODEL), SHARED_DIM ** -0.5),
        'final_norm_g': 1.0 + n(25, (D_MODEL,), 0.01),
    }

def reference(x_prompt, x_sample, state_ret_fwd, state_ret_bwd, c, c_ctx, w_ada, b_ada, norm1_g, norm2_g,
              w_in, ret_decay_fwd, ret_decay_bwd, ret_gn_g, w_four_out, w_ret_out, w_out, w_router, router_bias,
              w_exp_gate, w_exp_up, w_exp_down, w_shared_gate, w_shared_up, w_shared_down, final_norm_g):
    rope = _grid_rope(x_sample.shape[1])
    zeros = jnp.zeros((x_prompt.shape[0], N_RET_HEADS, RET_HEAD_DIM, RET_HEAD_DIM), jnp.float32)
    xc = x_prompt
    xs = x_sample
    new_f = []
    new_b = []
    for layer in range(DEPTH):
        lw = (w_ada[layer], b_ada[layer], norm1_g[layer], norm2_g[layer], w_in[layer], ret_decay_fwd[layer],
              ret_decay_bwd[layer], ret_gn_g[layer], w_four_out[layer], w_ret_out[layer], w_out[layer],
              w_router[layer], router_bias[layer], w_exp_gate[layer], w_exp_up[layer], w_exp_down[layer],
              w_shared_gate[layer], w_shared_up[layer], w_shared_down[layer])
        xc, s_f, s_b = _trunk_layer(xc, c_ctx[None, :], zeros, zeros, None, *lw)
        new_f.append(s_f)
        new_b.append(s_b)
        xs, _, _ = _trunk_layer(xs, c, state_ret_fwd[:, layer], state_ret_bwd[:, layer], rope, *lw)
    y_prompt = _rmsnorm(xc, final_norm_g)
    y_sample = _rmsnorm(xs, final_norm_g)
    new_state_fwd = jnp.stack(new_f, axis=1)
    new_state_bwd = jnp.stack(new_b, axis=1)
    return (y_prompt, y_sample, new_state_fwd, new_state_bwd)


_drawn_inputs = setup_inputs


def setup_inputs(seed=0):
    import zlib

    import numpy as np

    out = dict(_drawn_inputs(seed))
    spreads = {}
    factors = {'state_ret_fwd': 5.785,
     'state_ret_bwd': 4.86,
     'norm1_g': 5.297,
     'norm2_g': 3.075,
     'ret_gn_g': 6.639,
     'final_norm_g': 5.604}
    for name, (base, spread) in spreads.items():
        noise = np.random.default_rng([zlib.crc32(name.encode()), seed]).standard_normal(out[name].shape)
        drawn = base * np.exp(spread * noise) if base else spread * noise
        out[name] = __import__('jax').numpy.asarray(drawn.astype(out[name].dtype))
    for name, factor in factors.items():
        out[name] = (out[name] * factor).astype(out[name].dtype)
    return out
```

```python
import numpy as np
import concourse.bass as bass
from concourse import mybir
from concourse.alu_op_type import AluOpType as ALU
from contextlib import ExitStack

F32 = mybir.dt.float32
BF16 = mybir.dt.bfloat16
I32 = mybir.dt.int32
ACT = mybir.ActivationFunctionType
AX = mybir.AxisListType

P = 128
D = 1024
KC = D // P
CTX, LAT = 128, 256
T = CTX + LAT
TT = T // P
H = 4
RW = H * P
G = 8
E = 64
EG = 8
TOPG = 4
ED = 256
SLOTS = 64
EPS = 1e-6
ROUTED_SCALE = 2.5
GRID_W = 64
ROPE_BASE = 10000.0
ROWS = 2 * T + P
BIG = 3.0e38
CELL = 2048
PIECE = 2 * CELL
NPIECE_SLOTS = 6
NSLOT = 4
EXPERT = 3 * CELL
MAXOV = 64
BANKS = 8


def constants():
    a = np.arange
    parts = {}
    parts["ident"] = np.eye(P)
    c = 2 * np.pi * ((a(P)[:, None] * a(P)[None]) % P) / P
    parts["dft_chan"] = np.concatenate([np.cos(c), np.sin(c)], 1)
    n = (CTX * P) ** -0.5
    parts["dft_ctx"] = np.concatenate([np.cos(c) * n, -np.sin(c) * n], 1)
    w = 2 * np.pi * ((a(LAT)[:, None] * a(LAT)[None]) % LAT) / LAT
    n = (LAT * P) ** -0.5
    both = np.stack([np.cos(w) * n, -np.sin(w) * n], 1).reshape(2, P, 2 * LAT)
    parts["dft_lat"] = np.concatenate([both[0], both[1]], 1)
    nf = P // 4
    inv = np.float32(ROPE_BASE) ** (-a(nf, dtype=np.float32) / np.float32(nf))
    t = a(LAT)
    ar = (t // GRID_W).astype(np.float32)[:, None] * inv[None]
    ac = (t % GRID_W).astype(np.float32)[:, None] * inv[None]
    ang = np.concatenate([ar, ar, ac, ac], 1).astype(np.float64)
    sign = np.where((a(P) // nf) % 2 == 0, -1.0, 1.0)
    cos, sin = np.cos(ang), np.sin(ang) * sign
    parts["rope_cos"] = np.concatenate([cos[:P], cos[P:]], 1)
    parts["rope_sin"] = np.concatenate([sin[:P], sin[P:]], 1)
    parts["before"] = (a(P)[:, None] < a(P)[None]).astype(float)
    parts["slot"] = np.tile(a(SLOTS)[None], (P, 1))
    nr = T // SLOTS
    parts["tie"] = np.tile((a(EG)[None] < a(EG)[:, None]).astype(float).reshape(1, -1), (P, 1))
    parts["over"] = np.tile((SLOTS * a(1, nr))[None], (P, 1))
    p = a(P)
    cols = [p + 1, p + 1 + P, LAT - p, LAT - P - p, CTX - 1 - p, p,
            2 * T + p, p // SLOTS - p, p]
    parts["cols"] = np.stack(cols, 1)
    at, out, n = {}, [], 0
    for k, v in parts.items():
        at[k] = (n, n + v.shape[1])
        n += v.shape[1]
        out.append(v.astype(np.float32))
    return np.concatenate(out, 1), at


def distances():
    delta = np.arange(3 * P)[None] - P - np.arange(P)[:, None]
    return np.concatenate([np.maximum(delta, 0), np.maximum(-delta, 0)], 1).astype(np.float32)


CONST_AT = constants()[1]
NCONST = max(b for _, b in CONST_AT.values())

PIECES = (["ada2", "ada3", "ada0", "ada1"] + [f"win{i}" for i in range(6)]
          + ["win6", "four0", "win7", "four1", "win8", "win9", "ret", "ada4", "ada5", "out0", "out1",
             "ada8", "ada9", "ada6", "ada7", "ada10", "ada11", "sgu", "sd"])
PIECE_AT = {name: n for n, name in enumerate(PIECES)}


def psum_tiles():
    out = []

    def mod(name):
        out.extend((f"{name}{j}", "V") for j in range(2))
        out.extend((f"{name}_row{c}{j}", "A") for c in range(2) for j in range(2))

    mod("sc1")
    mod("sh1")
    for t in range(TT):
        out.extend([(f"h1T{t}0", "A"), (f"h1T{t}1", "V")])
    out.extend((f"uf{g}", "A") for g in range(G))
    for g in range(G + 1):
        if g < G:
            out.extend([(f"chan{g}a", "V"), (f"chan{g}b", "V")])
        if g > 0:
            out.append((f"pos{g - 1}", "A"))
    for n, eng in (("q", "V"), ("k", "V"), ("v", "A"), ("sw", "A")):
        out.extend((f"{n}{t}", eng) for t in range(TT))
    for t in range(TT):
        out.extend([(f"qT{t}", "A"), (f"kT{t}", "V")])
    out.extend([("state0", "A"), ("state1", "A"), ("sc_ctx", "V")])
    out.extend((f"sc_lat{h}", "V") for h in range(H))
    out.append(("o0", "V"))
    for t in (1, 2):
        out.extend([(f"o{t}", "V"), (f"cross_f{t}", "V"), (f"cross_b{t}", "V")])
    out.extend((f"retT{t}", "V") for t in range(TT))
    for m in range(KC):
        out.extend([(f"gf{m}", "A"), (f"fo{m}", "V")])
    for m in range(KC):
        out.extend([(f"gr{m}", "A"), (f"ro{m}", "V")])
    mod("g1")
    out.extend((f"mix{n}{t}", "V") for n in range(2) for t in range(TT))
    mod("sc2")
    mod("sh2")
    mod("g2")
    for t in range(TT):
        out.extend([(f"h2T{t}0", "A"), (f"h2T{t}1", "V")])
    out.append(("logits", "A"))
    out.extend((f"sgu{t}", "V") for t in range(TT))
    out.extend([("rank", "V"), ("count", "V"), ("start", "V"), ("table", "V")])
    out.extend((f"shT{t}", "A") for t in range(TT))
    out.extend((f"sd{t}{n}", "A") for t in range(TT) for n in range(2))
    out.append(("index", "A"))
    return out


TILES = psum_tiles()
TILE_AT = {name: n for n, (name, _) in enumerate(TILES)}
TURN = {}
for _n, (_name, _eng) in enumerate(TILES):
    TURN[_name] = sum(e == _eng for _, e in TILES[:_n + 1])
LAST_READ = {f"ada{i}": f"{name}{i % 2}" for name, i0 in (("sh1", 0), ("sc1", 2), ("g1", 4), ("sh2", 6), ("sc2", 8), ("g2", 10))
             for i in (i0, i0 + 1)}
LAST_READ |= {"win0": "uf3", "win1": "uf7", "win2": "q2", "win3": "k2", "win4": "v2", "win5": "sw2", "win6": "gf3",
              "four0": "fo3", "win7": "gf7", "four1": "fo7", "win8": "gr3", "win9": "gr7", "ret": "ro7",
              "out0": "mix02", "out1": "mix12", "sgu": "sgu2", "sd": "sd21"}
QUAD = 16


def trunk_kernel(nc, A, outs, consts, dists):
    y_prompt, y_sample, new_f, new_b = outs
    ctx = ExitStack()
    with ctx:
        def sb(name, shape, dt=F32):
            return ctx.enter_context(nc.sbuf_tensor(name, shape, dt))

        ring = sb("ring", [P, NSLOT * EXPERT])
        C = sb("consts_sb", [P, NCONST])
        x = sb("x", [P, TT, D])
        hT = sb("hT", [P, KC, T])
        U = sb("U", [P, 3072])
        Fm = sb("Fm", [P, 3072])
        VG = sb("VG", [P, 3072])
        QK = sb("QK", [P, 3072])
        DT = sb("DT", [P, H, 3 * P])
        MB = sb("MB", [P, 1024])
        S0 = sb("S0", [P, 2, H, P])
        AB = sb("AB", [P, 2, 768])
        work = sb("work", [P, 1024])
        small = sb("small", [P, 256])
        cond = sb("cond", [P, 2, KC])
        condr = sb("condr", [P, KC, 2])
        cbf = sb("cbf", [P, 3, P], BF16)
        idx = sb("idx", [P, E + MAXOV], I32)
        cw = sb("cw", [P, E + MAXOV])
        rows_now = sb("rows_now", [P, NSLOT], I32)
        tab = sb("tab", [1, 2 * MAXOV + 1], I32)
        ps = [ctx.enter_context(nc.psum_tensor(f"bank{i}", [P, 512], F32)) for i in range(BANKS)]
        h2_rows = nc.dram_tensor("h2_rows", [ROWS, 512], F32, kind="Internal").ap()
        y_rows = nc.dram_tensor("y_rows", [ROWS, 512], F32, kind="Internal").ap()

        sems = {}

        def sem(name):
            if name not in sems:
                sems[name] = ctx.enter_context(nc.semaphore(name))
            return sems[name]

        def const(name, rows=P):
            a, b = CONST_AT[name]
            return C[0:rows, a:b]

        ident = const("ident")
        cols = const("cols")

        uT = U[:, :].rearrange("p (g t) -> p g t", g=G)
        q_nat = U[:, 0:1536].rearrange("p (t n) -> p t n", t=TT)
        k_nat = U[:, 1536:3072].rearrange("p (t n) -> p t n", t=TT)
        sc_sb = U[:, 0:2560].rearrange("p (h n) -> p h n", h=5)
        mergedT = uT
        fmixT = Fm[:, :].rearrange("p (g t) -> p g t", g=G)
        v_nat = VG[:, 0:1536].rearrange("p (t n) -> p t n", t=TT)
        g_nat = VG[:, 1536:3072].rearrange("p (t n) -> p t n", t=TT)
        qT = QK[:, 0:1536].rearrange("p (h t) -> p h t", h=H)
        kT = QK[:, 1536:3072].rearrange("p (h t) -> p h t", h=H)
        retT = qT
        kw = AB[:, :, 0:512]
        lg = small[:, 0:8]
        pw = small[:, 8:32].rearrange("p (c h) -> p c h", c=6)
        ssq = small[:, 32:35]
        rstd = small[:, 35:38]
        dec = small[:, 40:48]
        gn_col = small[:, 48:52]
        s8 = small[:, 56:136].rearrange("p (n c) -> p n c", c=8)
        hst = small[:, 136:184].rearrange("p (n c) -> p n c", c=4)
        AB1 = AB[:, :, :].rearrange("p a b -> p (a b)")

        def rows_of(buf, at):
            return buf[:, at:at + 2048].rearrange("p (c n) -> p c n", c=2)

        DTf = DT[:, :, :].rearrange("p h n -> p (h n)")
        S0f = S0[:, :, :, :].rearrange("p a h e -> p (a h e)")
        wr = DTf[:, 1024:1536].rearrange("p (k e) -> p k e", k=KC)
        dist = U[:, 2048:2816]
        slot_ov = AB[:, :, :].rearrange("p a b -> p (a b)")[:, 1024:1408]
        tmpg = S0f[:, 0:2 * T].rearrange("p (b t) -> p b t", b=2)
        M6 = S0f[:, :].bitcast(BF16)[:, 0:TT * E * 6].rearrange("p (t e n) -> p t e n", t=TT, e=E)
        state_sb = MB[:, :].rearrange("p (d h e) -> p d h e", d=2, h=H)
        shT_sb = MB[:, 0:768].rearrange("p (t j q) -> p t j q", t=TT, j=2)
        junk = {1: VG[:, 2048:3072], 2: VG[:, 2048:3072], 3: Fm[:, 0:1024]}
        SECTION = {
            "sc1": (2, QK[0:2, 0:1024], QK[0:2, 1024:2048], QK[0:2, 2048:3072], rows_of(Fm, 0)),
            "sh1": (0, U[0:2, 0:1024], U[0:2, 1024:2048], None, rows_of(VG, 0)),
            "g1": (4, AB1[0:2, 0:1024], VG[0:2, 2048:3072], None, rows_of(VG, 0)),
            "sc2": (8, AB1[0:2, 0:1024], QK[0:2, 2048:3072], Fm[0:2, 2048:3072], rows_of(Fm, 0)),
            "sh2": (6, U[0:2, 2048:3072], DTf[0:2, 0:1024], None, rows_of(QK, 0)),
            "g2": (10, S0f[0:2, :], AB1[0:2, 0:1024], None, rows_of(U, 0)),
        }
        HN = {1: [Fm[:, 2048:3072], VG[:, 2048:3072], U[:, 2048:3072]],
              2: [VG[:, 0:1024], VG[:, 1024:2048], VG[:, 2048:3072]]}

        onehot = Fm[:, :].bitcast(BF16).rearrange("p (b c e s) -> p b c e s", b=2, c=TT, e=QUAD)
        xg = [QK[:, 0:512], QK[:, 512:1024]]
        xT = [QK[:, 1024:1536].rearrange("p (k s) -> p k s", k=4), QK[:, 1536:2048].rearrange("p (k s) -> p k s", k=4)]
        ysh = QK[:, 2048:3072]
        sg = [VG[:, 0:256], VG[:, 256:512]]
        hid = [VG[:, 512:768], VG[:, 768:1024]]
        hidT = [VG[:, 1024:1152].rearrange("p (j s) -> p j s", j=2), VG[:, 1152:1280].rearrange("p (j s) -> p j s", j=2)]
        yb = [VG[:, 1280:1792], VG[:, 1792:2304]]
        index_sb = VG[:, 2304:2688].rearrange("p (e n) -> p e n", n=6)
        ov_sb = VG[:, 2688:3072].rearrange("p (e n) -> p e n", n=6)
        s_silu = AB1[:, 0:256]
        s_hid = [AB1[:, 256:512], AB1[:, 512:768], AB1[:, 768:1024]]
        s_hidT = AB1[:, 1024:1280].rearrange("p (j t) -> p j t", j=2)
        fin_g = AB1[:, 0:1024]
        R = DTf.rearrange("p (n c e) -> p n c e", n=8, c=TT)
        r_score, r_bias, r_mask, r_rep, r_sel, r_w, r_rank, r_x = [R[:, n, :, :] for n in range(8)]
        rbf = sb("rbf", [E, 3 * MAXOV], BF16)
        ov_m6 = sb("ov_m6", [P, TT, 6], BF16)
        OVB = 0
        sel_bf = sb("sel_bf", [P, TT, E], BF16)
        bias_row = sb("bias_row", [P, E])
        rg = work[:, 0:512]

        w_ada = A["w_ada"].rearrange("o (p k) n -> (o p) k n", p=P)
        w_in = A["w_in"].rearrange("o (p k) n -> (o p) k n", p=P)
        w_four = A["w_four_out"].rearrange("o (k p) n -> (o p) k n", p=P)
        w_out = A["w_out"].rearrange("o (k p) n -> (o p) k n", p=P)
        w_ret = A["w_ret_out"].rearrange("o (k p) n -> (o p) k n", p=P)
        w_sg = A["w_shared_gate"].rearrange("o (p k) n -> (o p) k n", p=P)
        w_su = A["w_shared_up"].rearrange("o (p k) n -> (o p) k n", p=P)
        w_sd = A["w_shared_down"].rearrange("o (p k) n -> (o p) k n", p=P)
        w_eg = A["w_exp_gate"].rearrange("o e (p k) f -> (o e p) (k f)", p=P)
        w_eu = A["w_exp_up"].rearrange("o e (p k) f -> (o e p) (k f)", p=P)
        w_ed = A["w_exp_down"].rearrange("o e (p j) d -> (o e p) (j d)", p=P)
        b_ada = A["b_ada"]

        def piece(name):
            s = PIECE_AT[name] % NPIECE_SLOTS
            return ring[:, s * PIECE:(s + 1) * PIECE]

        def piece_landed(eng, name, parts=1):
            n = PIECE_AT[name]
            eng.wait_ge(sem(f"piece_slot{n % NPIECE_SLOTS}"), LANDED[name])

        LANDED, at = {}, [0] * NPIECE_SLOTS
        for n, name in enumerate(PIECES):
            at[n % NPIECE_SLOTS] += 32 if name == "sgu" else 16
            LANDED[name] = at[n % NPIECE_SLOTS]

        def expert(s):
            w = ring[:, s * EXPERT:(s + 1) * EXPERT]
            return (w[:, 0:CELL].rearrange("p (k f) -> p k f", k=KC),
                    w[:, CELL:2 * CELL].rearrange("p (k f) -> p k f", k=KC),
                    w[:, 2 * CELL:3 * CELL].rearrange("p (j d) -> p j d", j=2))

        def emptied(eng, name):
            eng.wait_ge(sem(f"emptied_{TILES[TILE_AT[name]][1]}"), TURN[name])

        def computed(eng, name):
            eng.wait_ge(sem("tile_done"), TILE_AT[name] + 1)

        for name in ("tile_done", "emptied_A", "emptied_V"):
            sem(name)

        block = ctx.enter_context(nc.Block())

        def stand_alone(eng, signal):
            eng.sem_inc(sem(signal), 1)

        def column(table, b):
            return table[:, b:b + 1] if isinstance(b, int) else table[:, bass.ds(b, 1)]

        def load_expert(sp, row, s):
            w = ring[:, s * EXPERT:(s + 1) * EXPERT]
            src = (lambda a: a[row:row + P, :]) if isinstance(row, int) else (lambda a: a[bass.ds(row, P), :])
            sp.dma_start(w[:, 0:CELL], src(w_eg)).then_inc(sem(f"gate_up_slot{s}"), 16)
            sp.dma_start(w[:, CELL:2 * CELL], src(w_eu)).then_inc(sem(f"gate_up_slot{s}"), 16)
            sp.dma_start(w[:, 2 * CELL:3 * CELL], src(w_ed)).then_inc(sem(f"down_slot{s}"), 16)

        @block.sync
        def _(sp):
            for n, name in enumerate(PIECES):
                dst = piece(name).rearrange("p (k n) -> p k n", k=KC)
                if n >= NPIECE_SLOTS:
                    computed(sp, LAST_READ[PIECES[n - NPIECE_SLOTS]])
                landed = sem(f"piece_slot{n % NPIECE_SLOTS}")
                if name.startswith("ada"):
                    i = int(name[3:])
                    sp.dma_start(dst, w_ada[:, :, i * 512:(i + 1) * 512]).then_inc(landed, 16)
                elif name.startswith("win"):
                    i = int(name[3:])
                    sp.dma_start(dst, w_in[:, :, i * 512:(i + 1) * 512]).then_inc(landed, 16)
                elif name.startswith("four"):
                    i = int(name[4:])
                    sp.dma_start(dst, w_four[:, :, i * 512:(i + 1) * 512]).then_inc(landed, 16)
                elif name.startswith("out"):
                    i = int(name[3:])
                    sp.dma_start(dst, w_out[:, :, i * 512:(i + 1) * 512]).then_inc(landed, 16)
                elif name == "ret":
                    sp.dma_start(piece(name).rearrange("p (k n) -> p k n", k=H), w_ret).then_inc(landed, 16)
                elif name == "sgu":
                    sp.dma_start(dst[:, :, 0:ED], w_sg).then_inc(landed, 16)
                    sp.dma_start(dst[:, :, ED:2 * ED], w_su).then_inc(landed, 16)
                else:
                    sp.dma_start(piece(name)[:, 0:CELL].rearrange("p (k n) -> p k n", k=2), w_sd).then_inc(landed, 16)
            last = len(PIECES)
            for s in range(NSLOT):
                lo, hi = s * EXPERT // PIECE, ((s + 1) * EXPERT - 1) // PIECE
                need = max(n for n in range(last) if lo <= n % NPIECE_SLOTS <= hi)
                computed(sp, LAST_READ[PIECES[need]])
                load_expert(sp, s * P, s)
            with sp.Fori(1, E // NSLOT) as i:
                for s in range(NSLOT):
                    sp.wait_ge(sem("down_done"), i * NSLOT + (s - NSLOT + 1))
                    load_expert(sp, i * (NSLOT * P) + s * P, s)
            sp.wait_ge(sem("table_ready"), 1)
            n2 = sp.value_load(tab[0:1, 2 * MAXOV:2 * MAXOV + 1], min_val=0, max_val=MAXOV // 2)
            with sp.If(n2 > 0):
                with sp.Fori(0, n2) as i:
                    for s in range(2):
                        e = sp.value_load(tab[0:1, bass.ds(i * 2 + s, 1)], min_val=0, max_val=E - 1)
                        sp.wait_ge(sem("down_done"), i * 2 + (E + s - 1))
                        load_expert(sp, e * P, s)
            sp.nop()
            for t in range(TT):
                sp.wait_ge(sem("out_ready"), t + 1)
                dst = y_prompt[0, :, :] if t == 0 else y_sample[0, (t - 1) * P:t * P, :]
                sp.dma_start(dst, x[:, t, :]).then_inc(sem("out_written"), 16)
            sp.wait_ge(sem("out_written"), 16 * TT)

        def gather(pool, b, s):
            nc.gpsimd.tensor_copy(rows_now[:, s:s + 1], column(idx, b)).then_inc(sem("rows_now_ready"), 1)
            pool.wait_ge(sem("rows_now_ready"), b + 1)
            stand_alone(pool, "pool_passed")
            pool.indirect_dma_start(xg[s % 2], None, h2_rows, bass.IndirectOffsetOnAxis(rows_now[:, s:s + 1], 0),
                                    bounds_check=ROWS - 1).then_inc(sem(f"gathered{s % 2}"), 16)

        def scatter_add(pool, s):
            stand_alone(pool, "pool_passed")
            pool.indirect_dma_start(y_rows, bass.IndirectOffsetOnAxis(rows_now[:, s:s + 1], 0), yb[s % 2], None,
                                    bounds_check=ROWS - 1, compute_op=ALU.add).then_inc(sem("scattered"), 16)


        @block.gpsimd
        def _(pool):
            pool.dma_start(C[:, :], consts).then_inc(sem("consts_in"), 16)
            pool.dma_start(cond[:, 0, :], A["c_ctx"].rearrange("(p k) -> p k", p=P)).then_inc(sem("cond_in"), 16)
            pool.dma_start(cond[:, 1, :], A["c"].rearrange("o (p k) -> (o p) k", p=P)).then_inc(sem("cond_in"), 16)

            def bias_rows(name):
                i, _, bias, gain, _ = SECTION[name]
                pool.dma_start(bias, b_ada[0:1, i * 512:i * 512 + D].broadcast_to([2, D])).then_inc(sem(f"{name}_bias_in"), 16)
                if gain is not None:
                    g = A["norm1_g"] if name == "sc1" else A["norm2_g"]
                    pool.dma_start(gain, g[0:1, :].broadcast_to([2, D])).then_inc(sem(f"{name}_bias_in"), 16)

            bias_rows("sc1")
            bias_rows("sh1")
            pool.dma_start(x[:, 0, :], A["x_prompt"][0, :, :]).then_inc(sem("x_in"), 16)
            pool.dma_start(x[:, 1:3, :], A["x_sample"][0, :, :].rearrange("(t p) d -> p t d", p=P)).then_inc(sem("x_in"), 16)
            pool.dma_start(dist, dists).then_inc(sem("dist_in"), 16)
            pool.dma_start(dec[:, 0:4], A["ret_decay_fwd"][0:1, :].broadcast_to([P, H])).then_inc(sem("decay_in"), 16)
            pool.dma_start(dec[:, 4:8], A["ret_decay_bwd"][0:1, :].broadcast_to([P, H])).then_inc(sem("decay_in"), 16)
            pool.dma_start(S0[:, 0, :, :], A["state_ret_fwd"][0, 0].rearrange("h d e -> d h e")).then_inc(sem("state_in"), 16)
            pool.dma_start(S0[:, 1, :, :], A["state_ret_bwd"][0, 0].rearrange("h d e -> d h e")).then_inc(sem("state_in"), 16)
            pool.dma_start(gn_col, A["ret_gn_g"].rearrange("o (h p) -> (o p) h", p=P), allow_slow_non_contiguous=True).then_inc(sem("gn_in"), 16)
            pool.dma_start(bias_row[:, :], A["router_bias"][0:1, :].broadcast_to([P, E])).then_inc(sem("router_in"), 16)
            nc.gpsimd.memset(AB1[:, 0:512], 0.0).then_inc(sem("zeros"), 1)
            pool.wait_ge(sem("zeros"), 1)
            pool.dma_start(h2_rows[2 * T:ROWS, :], AB1[:, 0:512]).then_inc(sem("pads_written"), 16)
            pool.dma_start(y_rows[2 * T:ROWS, :], AB1[:, 0:512]).then_inc(sem("pads_written"), 16)
            pool.wait_ge(sem("pads_written"), 32)

            emptied(pool, "state1")
            pool.dma_start(new_f[0, 0].rearrange("h d e -> d h e"), state_sb[:, 0, :, :]).then_inc(sem("states_written"), 16)
            pool.dma_start(new_b[0, 0].rearrange("h d e -> d h e"), state_sb[:, 1, :, :]).then_inc(sem("states_written"), 16)
            pool.wait_ge(sem("states_written"), 32)
            computed(pool, "retT2")
            bias_rows("g1")
            computed(pool, "ro7")
            pool.dma_start(wr, A["w_router"].rearrange("o (p k) e -> (o p) k e", p=P)).then_inc(sem("router_in"), 16)
            bias_rows("sc2")
            bias_rows("sh2")
            computed(pool, "sc2_row11")
            bias_rows("g2")
            for t in range(TT):
                pool.wait_ge(sem("h2_ready"), t + 1)
                pool.dma_start(h2_rows[2 * t * P:2 * (t + 1) * P, :].rearrange("(p j) n -> p (j n)", j=2),
                               HN[2][t]).then_inc(sem("h2_written"), 16)
            for t in range(TT):
                emptied(pool, f"sd{t}1")
                pool.dma_start(y_rows[2 * t * P:2 * (t + 1) * P, :].rearrange("(p j) n -> p (j n)", j=2),
                               ysh).then_inc(sem("y_started"), 16)
                pool.wait_ge(sem("y_started"), 16 * (t + 1))
            pool.dma_start(fin_g, A["final_norm_g"].rearrange("(o n) -> o n", o=1).broadcast_to([P, D])).then_inc(sem("fin_in"), 16)
            pool.wait_ge(sem("h2_written"), 16 * TT)

            pool.wait_ge(sem("index_ready"), 1)
            gather(pool, 0, 0)
            gather(pool, 1, 1)

            def step(b, s, more):
                if more:
                    pool.wait_ge(sem("tokens_used"), b + 1)
                    stand_alone(pool, "pool_passed")
                    gather(pool, b + 2, (s + 2) % NSLOT)
                pool.wait_ge(sem("y_ready"), b + 1)
                if not (isinstance(b, int) and b == 0):
                    pool.wait_ge(sem("scattered"), b * 16)
                scatter_add(pool, s)

            for b in range(NSLOT):
                step(b, b, True)
            with pool.Fori(1, E // NSLOT - 1) as i:
                for s in range(NSLOT):
                    step(i * NSLOT + s, s, True)
            for b in range(E - NSLOT, E):
                step(b, b % NSLOT, b + 2 < E)
            pool.wait_ge(sem("overflow_index_ready"), 1)
            n2 = pool.value_load(tab[0:1, 2 * MAXOV:2 * MAXOV + 1], min_val=0, max_val=MAXOV // 2)
            with pool.If(n2 > 0):
                with pool.Fori(0, n2) as i:
                    for s in range(2):
                        b = i * 2 + (E + s)
                        pool.wait_ge(sem("tokens_used"), b - 1)
                        stand_alone(pool, "pool_passed")
                        gather(pool, b, s)
                        pool.wait_ge(sem("y_ready"), b + 1)
                        pool.wait_ge(sem("scattered"), b * 16)
                        scatter_add(pool, s)
            pool.wait_ge(sem("scattered"), n2 * 32 + 16 * E)
            stand_alone(pool, "pool_passed")
            for t in range(TT):
                pool.dma_start(hT[:, :, :].rearrange("p k t -> p (k t)")[:, t * D:(t + 1) * D],
                               y_rows[2 * t * P:2 * (t + 1) * P, :].rearrange("(p j) n -> p (j n)", j=2)).then_inc(sem(f"y_in{t}"), 16)

        @block.tensor
        def _(pe):
            mm = nc.tensor.matmul
            turn = [0]

            def bank(name):
                n = TILE_AT[name]
                assert n == turn[0], (name, TILES[turn[0]])
                turn[0] += 1
                if n >= BANKS:
                    before, eng = TILES[n - BANKS]
                    pe.wait_ge(sem(f"emptied_{eng}"), TURN[before])
                return ps[n % BANKS]

            def done(ins):
                ins.then_inc(sem("tile_done"), 1)

            def section(name):
                i, row, _, _, _ = SECTION[name]
                for j in range(2):
                    w = piece(f"ada{i + j}").rearrange("p (k n) -> p k n", k=KC)
                    o = bank(f"{name}{j}")
                    piece_landed(pe, f"ada{i + j}")
                    for k in range(KC):
                        ins = mm(o[0:2, :], condr[:, k, :], w[:, k, :], start=(k == 0), stop=(k == KC - 1))
                    done(ins)
                if SECTION[name][3] is None:
                    emptied(pe, f"{name}1")
                else:
                    pe.wait_ge(sem(f"{name}_row"), 2)
                for c in range(2):
                    for j in range(2):
                        o = bank(f"{name}_row{c}{j}")
                        done(mm(o[:, :], ident[0:2, c:c + 1].broadcast_to([2, P]), row[:, j * 512:(j + 1) * 512], start=True, stop=True))

            pe.wait_ge(sem("consts_in"), 16)
            pe.wait_ge(sem("cond_ready"), 1)
            section("sc1")
            section("sh1")

            def transposed(n):
                for t in range(TT):
                    pe.wait_ge(sem(f"h{n}_ready"), t + 1)
                    for half in range(2):
                        o = bank(f"h{n}T{t}{half}")
                        for k in range(4):
                            kk = half * 4 + k
                            ins = nc.tensor.transpose(o[:, k * P:(k + 1) * P], HN[n][t][:, kk * P:(kk + 1) * P], ident)
                        done(ins)

            transposed(1)
            emptied(pe, "h1T20")
            emptied(pe, "h1T21")

            def features(tile, w, m, rhs, kc):
                o = bank(tile)
                for k in range(kc):
                    ins = mm(o[:, 0:T], w[:, k, m * P:(m + 1) * P], rhs[:, k, :], start=(k == 0), stop=(k == kc - 1))
                done(ins)

            for g in range(G):
                if g % 4 == 0:
                    piece_landed(pe, f"win{g // 4}")
                features(f"uf{g}", piece(f"win{g // 4}").rearrange("p (k n) -> p k n", k=KC), g % 4, hT, KC)

            for g in range(G + 1):
                if g < G:
                    emptied(pe, f"uf{g}")
                    for tiles, part in (((0, 1), "a"), ((2,), "b")):
                        o = bank(f"chan{g}{part}")
                        for n, t in enumerate(tiles):
                            ins = mm(o[:, n * 256:(n + 1) * 256], uT[:, g, t * P:(t + 1) * P], const("dft_chan"), start=True, stop=True)
                        done(ins)
                if g > 0:
                    gg = g - 1
                    emptied(pe, f"chan{gg}b")
                    a = AB[:, gg % 2, :].rearrange("p (t n) -> p t n", t=TT)
                    o = bank(f"pos{gg}")
                    cctx = const("dft_ctx")
                    clat = const("dft_lat")
                    for s in range(2):
                        mm(o[:, 0:CTX], a[:, 0, s * P:(s + 1) * P], cctx[:, s * P:(s + 1) * P], start=(s == 0), stop=(s == 1))
                    for n in range(4):
                        tc, s = n // 2, n % 2
                        ins = mm(o[:, CTX:T], a[:, 1 + tc, s * P:(s + 1) * P], clat[:, n * LAT:(n + 1) * LAT], start=(n == 0), stop=(n == 3))
                    done(ins)

            for i, name in enumerate(("q", "k", "v", "sw")):
                w = piece(f"win{2 + i}").rearrange("p (k n) -> p k n", k=KC)
                piece_landed(pe, f"win{2 + i}")
                for t in range(TT):
                    o = bank(f"{name}{t}")
                    for k in range(KC):
                        ins = mm(o[:, :], hT[:, k, t * P:(t + 1) * P], w[:, k, :], start=(k == 0), stop=(k == KC - 1))
                    done(ins)

            for t in range(TT):
                for name, nat in (("q", q_nat), ("k", k_nat)):
                    if t:
                        pe.wait_ge(sem(f"{name}_rotated"), t)
                    else:
                        emptied(pe, f"{name}0")
                    o = bank(f"{name}T{t}")
                    for h in range(H):
                        ins = nc.tensor.transpose(o[:, h * P:(h + 1) * P], nat[:, t, h * P:(h + 1) * P], ident)
                    done(ins)
            emptied(pe, "v2")
            for d in range(2):
                pe.wait_ge(sem("kw_ready"), d + 1)
                o = bank(f"state{d}")
                for h in range(H):
                    ins = mm(o[:, h * P:(h + 1) * P], kw[:, d, h * P:(h + 1) * P], v_nat[:, 0, h * P:(h + 1) * P], start=True, stop=True)
                done(ins)
            emptied(pe, "qT2")
            emptied(pe, "kT2")
            o = bank("sc_ctx")
            for h in range(H):
                ins = mm(o[:, h * P:(h + 1) * P], kT[:, h, 0:P], qT[:, h, 0:P], start=True, stop=True)
            done(ins)
            for h in range(H):
                o = bank(f"sc_lat{h}")
                for j in range(2):
                    ins = mm(o[:, j * LAT:(j + 1) * LAT], kT[:, h, (1 + j) * P:(2 + j) * P], qT[:, h, CTX:T], start=True, stop=True)
                done(ins)
            emptied(pe, "sc_ctx")
            o = bank("o0")
            for h in range(H):
                ins = mm(o[:, h * P:(h + 1) * P], sc_sb[:, 4, h * P:(h + 1) * P], v_nat[:, 0, h * P:(h + 1) * P], start=True, stop=True)
            done(ins)
            pe.wait_ge(sem("state_in"), 32)
            for t in (1, 2):
                o = bank(f"o{t}")
                for h in range(H):
                    emptied(pe, f"sc_lat{h}")
                    for j in range(2):
                        ins = mm(o[:, h * P:(h + 1) * P], sc_sb[:, h, j * LAT + (t - 1) * P:j * LAT + t * P],
                                 v_nat[:, 1 + j, h * P:(h + 1) * P], start=(j == 0), stop=(j == 1))
                done(ins)
                for d, name in ((0, "cross_f"), (1, "cross_b")):
                    o = bank(f"{name}{t}")
                    for h in range(H):
                        ins = mm(o[:, h * P:(h + 1) * P], qT[:, h, t * P:(t + 1) * P], S0[:, d, h, :], start=True, stop=True)
                    done(ins)
            for t in range(TT):
                pe.wait_ge(sem("ret_ready"), t + 1)
                o = bank(f"retT{t}")
                for h in range(H):
                    ins = nc.tensor.transpose(o[:, h * P:(h + 1) * P], g_nat[:, t, h * P:(h + 1) * P], ident)
                done(ins)

            emptied(pe, "pos7")
            for m in range(KC):
                i = m // 4
                if m % 4 == 0:
                    piece_landed(pe, f"win{6 + i}")
                    piece_landed(pe, f"four{i}")
                features(f"gf{m}", piece(f"win{6 + i}").rearrange("p (k n) -> p k n", k=KC), m % 4, hT, KC)
                features(f"fo{m}", piece(f"four{i}").rearrange("p (k n) -> p k n", k=KC), m % 4, fmixT, G)
            emptied(pe, "retT2")
            for m in range(KC):
                i = m // 4
                if m % 4 == 0:
                    piece_landed(pe, f"win{8 + i}")
                if m == 0:
                    piece_landed(pe, "ret")
                features(f"gr{m}", piece(f"win{8 + i}").rearrange("p (k n) -> p k n", k=KC), m % 4, hT, KC)
                features(f"ro{m}", piece("ret").rearrange("p (k n) -> p k n", k=H), m, retT, H)

            section("g1")
            pe.wait_ge(sem("merged"), KC)
            for n in range(2):
                w = piece(f"out{n}").rearrange("p (k n) -> p k n", k=KC)
                piece_landed(pe, f"out{n}")
                for t in range(TT):
                    o = bank(f"mix{n}{t}")
                    for k in range(KC):
                        ins = mm(o[:, :], mergedT[:, k, t * P:(t + 1) * P], w[:, k, :], start=(k == 0), stop=(k == KC - 1))
                    done(ins)
            section("sc2")
            section("sh2")
            section("g2")
            transposed(2)
            emptied(pe, "h2T20")
            emptied(pe, "h2T21")
            pe.wait_ge(sem("router_in"), 32)
            o = bank("logits")
            for t in range(TT):
                for k in range(KC):
                    ins = mm(o[:, t * E:(t + 1) * E], hT[:, k, t * P:(t + 1) * P], wr[:, k, :], start=(k == 0), stop=(k == KC - 1))
            done(ins)
            piece_landed(pe, "sgu")
            w = piece("sgu").rearrange("p (k n) -> p k n", k=KC)
            for t in range(TT):
                o = bank(f"sgu{t}")
                for k in range(KC):
                    ins = mm(o[:, :], hT[:, k, t * P:(t + 1) * P], w[:, k, :], start=(k == 0), stop=(k == KC - 1))
                done(ins)
            pe.wait_ge(sem("cbf_ready"), 3)
            pe.wait_ge(sem("sel_ready"), 1)
            o = bank("rank")
            for t in range(TT):
                for u in range(t + 1):
                    ins = mm(o[:, t * E:(t + 1) * E], cbf[:, 0 if u == t else 1, :], sel_bf[:, u, :], start=(u == 0), stop=(u == t))
            done(ins)
            o = bank("count")
            for t in range(TT):
                ins = mm(o[0:E, 0:1], sel_bf[:, t, :], cbf[:, 1, 0:1], start=(t == 0), stop=(t == TT - 1))
            done(ins)
            pe.wait_ge(sem("further_ready"), 1)
            done(mm(bank("start")[0:E, 0:1], cbf[0:E, 0, 0:E], rbf[0:E, 0:1], start=True, stop=True))
            pe.wait_ge(sem("blocks_ready"), 1)
            o = bank("table")
            mm(o[0:1, 0:MAXOV], cbf[0:E, 2, 0:1], rbf[0:E, MAXOV:2 * MAXOV], start=True, stop=True)
            mm(o[0:1, MAXOV:2 * MAXOV], cbf[0:E, 1, 0:1], rbf[0:E, 2 * MAXOV:3 * MAXOV], start=True, stop=True)
            done(mm(o[0:1, 2 * MAXOV:3 * MAXOV], cbf[0:E, 1, 0:1], rbf[0:E, MAXOV:2 * MAXOV], start=True, stop=True))
            for t in range(TT):
                emptied(pe, f"sgu{t}")
                o = bank(f"shT{t}")
                for j in range(2):
                    ins = nc.tensor.transpose(o[:, j * P:(j + 1) * P], s_hid[t][:, j:ED:2], ident)
                done(ins)
            piece_landed(pe, "sd")
            w = piece("sd")[:, 0:CELL].rearrange("p (j n) -> p j n", j=2)
            for t in range(TT):
                emptied(pe, f"shT{t}")
                for n in range(2):
                    o = bank(f"sd{t}{n}")
                    for j in range(2):
                        ins = mm(o[:, :], shT_sb[:, t, j, :], w[:, j, n * 512:(n + 1) * 512], start=(j == 0), stop=(j == 1))
                    done(ins)

            o = bank("index")
            pe.wait_ge(sem("m6_ready"), 1)
            for q in range(E // QUAD):
                pe.wait_ge(sem("onehot_ready"), q + 1)
                for e in range(QUAD):
                    ee = q * QUAD + e
                    for t in range(TT):
                        for half in range(2):
                            ins = mm(o[half * SLOTS:(half + 1) * SLOTS, ee * 6:ee * 6 + 6], onehot[:, q % 2, t, e, :],
                                     M6[:, t, ee, :], start=(t == 0), stop=(t == TT - 1))
                if q < E // QUAD - 1:
                    ins.then_inc(sem("onehot_used"), 1)
            done(ins)
            emptied(pe, "index")
            emptied(pe, "table")
            pe.wait_ge(sem("table_ready"), 1)
            n2 = pe.value_load(tab[0:1, 2 * MAXOV:2 * MAXOV + 1], min_val=0, max_val=MAXOV // 2)
            with pe.If(n2 > 0):
                with pe.Fori(0, n2 * 2) as i:
                    pe.wait_ge(sem("ov_step"), i * (2 * TT) + 2 * TT)
                    for t in range(TT):
                        for half in range(2):
                            ins = mm(ps[OVB][half * SLOTS:(half + 1) * SLOTS, 0:6], onehot[:, 0, t, 0, :], ov_m6[:, t, :],
                                     start=(t == 0), stop=(t == TT - 1))
                    ins.then_inc(sem("ov_index_done"), 1)
            pe.nop()


            def tokens(b, par, turn):
                pe.wait_ge(sem(f"gathered{par}"), turn)
                if not (isinstance(b, int) and b < 2):
                    pe.wait_ge(sem("xT_ready"), b - 1)
                for k in range(4):
                    ins = nc.tensor.transpose(ps[4 + par][:, k * P:(k + 1) * P], xg[par][:, k * P:(k + 1) * P], ident)
                ins.then_inc(sem("tokens_used"), 1)

            def gate_up(b, s, uses):
                par = s % 2
                wg, wu, _ = expert(s)
                pe.wait_ge(sem("xT_ready"), b + 1)
                pe.wait_ge(sem(f"gate_up_slot{s}"), uses)
                if not (isinstance(b, int) and b < 2):
                    pe.wait_ge(sem("hid_ready"), b - 1)
                for k in range(KC):
                    lhs = xT[par][:, k % 4, (k // 4) * SLOTS:(k // 4 + 1) * SLOTS]
                    mm(ps[par][0:SLOTS, 0:ED], lhs, wg[:, k, :], start=(k == 0), stop=(k == KC - 1))
                    ins = mm(ps[par][SLOTS:P, 0:ED], lhs, wu[:, k, :], start=(k == 0), stop=(k == KC - 1))
                ins.then_inc(sem("gate_up_done"), 1)

            def hidden_T(b, par):
                pe.wait_ge(sem("hid_ready"), b + 1)
                if not (isinstance(b, int) and b < 2):
                    pe.wait_ge(sem("hidT_ready"), b - 1)
                stand_alone(pe, "pe_passed")
                for j in range(2):
                    ins = nc.tensor.transpose(ps[6 + par][:, j * SLOTS:(j + 1) * SLOTS], hid[par][SLOTS:P, j:ED:2], ident[SLOTS:P, SLOTS:P])
                ins.then_inc(sem("hidT_done"), 1)

            def down(b, s, uses):
                par = s % 2
                _, _, wd = expert(s)
                pe.wait_ge(sem("hidT_ready"), b + 1)
                pe.wait_ge(sem(f"down_slot{s}"), uses)
                if not (isinstance(b, int) and b < 2):
                    pe.wait_ge(sem("y_ready"), b - 1)
                for j in range(2):
                    mm(ps[2 + par][0:SLOTS, :], hidT[par][:, j, :], wd[:, j, 0:512], start=(j == 0), stop=(j == 1))
                    ins = mm(ps[2 + par][SLOTS:P, :], hidT[par][:, j, :], wd[:, j, 512:1024], start=(j == 0), stop=(j == 1))
                ins.then_inc(sem("down_done"), 1)

            def step(b, i, s, more):
                gate_up(b, s, i * 32 + 32)
                if not (isinstance(b, int) and b == 0):
                    down(b - 1, (s - 1) % NSLOT, i * 16 + (16 if s else 0))
                hidden_T(b, s % 2)
                if more:
                    tokens(b + 1, (s + 1) % 2, i * 32 + 16 * ((s + 1) // 2) + 16)

            tokens(0, 0, 16)
            for b in range(NSLOT):
                step(b, 0, b, True)
            with pe.Fori(1, E // NSLOT - 1) as i:
                for s in range(NSLOT):
                    step(i * NSLOT + s, i, s, True)
            for b in range(E - NSLOT, E):
                step(b, E // NSLOT - 1, b % NSLOT, b + 1 < E)
            down(E - 1, NSLOT - 1, 16 * (E // NSLOT))
            with pe.If(n2 > 0):
                with pe.Fori(0, n2) as i:
                    for s in range(2):
                        b = i * 2 + (E + s)
                        tokens(b, s, i * 16 + 16 * (E // 2 + 1))
                        gate_up(b, s, i * 32 + 32 * (E // NSLOT + 1))
                        hidden_T(b, s)
                        down(b, s, i * 16 + 16 * (E // NSLOT + 1))
            pe.nop()


        @block.scalar
        def _(act):
            chain = [0]
            turns = [0]

            def link(ins):
                chain[0] += 1
                ins.then_inc(sem("act_chain"), 1)
                act.wait_ge(sem("act_chain"), chain[0])

            def tile(name):
                act.wait_ge(sem("tile_done"), TILE_AT[name] + 1)
                return ps[TILE_AT[name] % BANKS]

            def emptied_by(ins, name):
                assert TURN[name] == turns[0] + 1, name
                turns[0] += 1
                ins.then_inc(sem("emptied_A"), 1)

            def spread(name):
                rows = SECTION[name][4]
                for c in range(2):
                    for j in range(2):
                        n = f"{name}_row{c}{j}"
                        o = tile(n)
                        emptied_by(nc.scalar.copy(rows[:, c, j * 512:(j + 1) * 512], o[:, :]), n)

            act.wait_ge(sem("cond_in"), 32)
            nc.scalar.activation(condr[:, :, :].rearrange("p k c -> p c k"), cond[:, :, :], ACT.Silu).then_inc(sem("cond_ready"), 1)
            act.wait_ge(sem("x_in"), 32)
            for t in range(TT):
                if t:
                    act.wait_ge(sem("ssq1"), t)
                nc.scalar.activation(junk[1], x[:, t, :], ACT.Square, accum_out=ssq[:, t:t + 1]).then_inc(sem("ssq1"), 1)
            act.wait_ge(sem("dec_abs"), 1)
            nc.scalar.activation(s8[:, 1, :], s8[:, 0, :], ACT.Exp, scale=-1.0).then_inc(sem("dec_exp"), 1)
            act.wait_ge(sem("dec_u"), 1)
            nc.scalar.activation(s8[:, 3, :], s8[:, 2, :], ACT.Ln).then_inc(sem("dec_ln"), 1)
            act.wait_ge(sem("dec_args"), 1)
            nc.scalar.activation(DTf, DTf, ACT.Exp).then_inc(sem("decays"), 1)
            nc.scalar.activation(pw, pw, ACT.Exp).then_inc(sem("decays"), 1)
            act.wait_ge(sem("var1"), 1)
            nc.scalar.activation(rstd, rstd, ACT.Sqrt).then_inc(sem("std1"), 1)
            spread("sc1")
            spread("sh1")

            def hT_half(n):
                for t in range(TT):
                    name = f"h{n}T{t}0"
                    o = tile(name)
                    emptied_by(nc.scalar.copy(hT[:, 0:4, t * P:(t + 1) * P], o[:, :].rearrange("p (k t) -> p k t", k=4)), name)

            hT_half(1)
            for g in range(G):
                name = f"uf{g}"
                o = tile(name)
                emptied_by(nc.scalar.copy(uT[:, g, :], o[:, 0:T]), name)
            for g in range(G):
                name = f"pos{g}"
                o = tile(name)
                emptied_by(nc.scalar.copy(fmixT[:, g, :], o[:, 0:T]), name)
            for t in range(TT):
                o = tile(f"v{t}")
                emptied_by(nc.scalar.copy(v_nat[:, t, :], o[:, :]), f"v{t}")
            for t in range(TT):
                o = tile(f"sw{t}")
                emptied_by(nc.scalar.activation(g_nat[:, t, :], o[:, :], ACT.Silu), f"sw{t}")
            for t in range(TT):
                o = tile(f"qT{t}")
                emptied_by(nc.scalar.mul(qT[:, :, t * P:(t + 1) * P], o[:, :].rearrange("p (h t) -> p h t", h=H), float(P) ** -0.5), f"qT{t}")
            for d in range(2):
                o = tile(f"state{d}")
                emptied_by(nc.scalar.copy(state_sb[:, d, :, :], o[:, :].rearrange("p (h e) -> p h e", h=H)), f"state{d}")
            for t in range(TT):
                act.wait_ge(sem("head_var"), t + 1)
                nc.scalar.activation(hst[:, 3 * t + 1, :], hst[:, 3 * t + 1, :], ACT.Sqrt).then_inc(sem("head_std"), 1)
            for kind in ("gf", "gr"):
                for m in range(KC):
                    n = m + (KC if kind == "gr" else 0)
                    if n >= 2:
                        emptied(act, f"{'fo' if n - 2 < KC else 'ro'}{(n - 2) % KC}")
                    o = tile(f"{kind}{m}")
                    emptied_by(nc.scalar.activation(tmpg[:, m % 2, :], o[:, 0:T], ACT.Sigmoid), f"{kind}{m}")
            spread("g1")
            spread("sc2")
            spread("sh2")
            spread("g2")
            for t in range(TT):
                act.wait_ge(sem("x1_ready"), t + 1)
                if t:
                    act.wait_ge(sem("ssq2"), t)
                nc.scalar.activation(junk[2], x[:, t, :], ACT.Square, accum_out=ssq[:, t:t + 1]).then_inc(sem("ssq2"), 1)
            act.wait_ge(sem("var2"), 1)
            nc.scalar.activation(rstd, rstd, ACT.Sqrt).then_inc(sem("std2"), 1)
            hT_half(2)
            o = tile("logits")
            emptied_by(nc.scalar.activation(r_score, o[:, 0:TT * E].rearrange("p (t e) -> p t e", t=TT), ACT.Sigmoid), "logits")
            for t in range(TT):
                o = tile(f"sgu{t}")
                if t:
                    emptied(act, f"sgu{t - 1}")
                nc.scalar.activation(s_silu, o[:, 0:ED], ACT.Silu).then_inc(sem("ssilu_ready"), 1)
            for t in range(TT):
                o = tile(f"shT{t}")
                emptied_by(nc.scalar.copy(shT_sb[:, t, :, :], o[:, 0:ED].rearrange("p (j t) -> p j t", j=2)), f"shT{t}")
            for t in range(TT):
                if t:
                    act.wait_ge(sem("y_started"), 16 * t)
                for n in range(2):
                    o = tile(f"sd{t}{n}")
                    emptied_by(nc.scalar.copy(ysh[:, n * 512:(n + 1) * 512], o[:, :]), f"sd{t}{n}")
            act.wait_ge(sem("h2_written"), 16 * TT)
            o = tile("index")
            emptied_by(nc.scalar.copy(index_sb, o[:, 0:E * 6].rearrange("p (e n) -> p e n", n=6)), "index")
            act.wait_ge(sem("index_ready"), 1)

            def silu(b, par):
                act.wait_ge(sem("gate_up_done"), b + 1)
                if not (isinstance(b, int) and b < 2):
                    act.wait_ge(sem("hid_ready"), b - 1)
                nc.scalar.activation(sg[par][SLOTS:P, :], ps[par][0:SLOTS, 0:ED], ACT.Silu).then_inc(sem("silu_ready"), 1)

            def outputs(b, par):
                act.wait_ge(sem("down_done"), b + 1)
                if not (isinstance(b, int) and b < 2):
                    act.wait_ge(sem("scattered"), b * 16 - 16)
                nc.scalar.activation(yb[par], ps[2 + par][:, :], ACT.Copy, scale=column(cw, b)).then_inc(sem("y_ready"), 1)

            def step(b, s):
                silu(b, s % 2)
                if not (isinstance(b, int) and b == 0):
                    outputs(b - 1, (s - 1) % 2)

            for b in range(NSLOT):
                step(b, b)
            with act.Fori(1, E // NSLOT) as i:
                for s in range(NSLOT):
                    step(i * NSLOT + s, s)
            outputs(E - 1, (E - 1) % 2)
            act.wait_ge(sem("overflow_index_ready"), 1)
            n2 = act.value_load(tab[0:1, 2 * MAXOV:2 * MAXOV + 1], min_val=0, max_val=MAXOV // 2)
            with act.If(n2 > 0):
                with act.Fori(0, n2) as i:
                    for s in range(2):
                        silu(i * 2 + (E + s), s)
                        outputs(i * 2 + (E + s), s)
            act.nop()
            for t in range(TT):
                act.wait_ge(sem("x2_ready"), t + 1)
                nc.scalar.activation(junk[3], x[:, t, :], ACT.Square, accum_out=ssq[:, t:t + 1]).then_inc(sem("ssq3"), 1)
                act.wait_ge(sem("var3"), t + 1)
                nc.scalar.activation(rstd[:, t:t + 1], rstd[:, t:t + 1], ACT.Sqrt).then_inc(sem("std3"), 1)

        @block.vector
        def _(dve):
            v = nc.vector
            chain = [0]
            turns = [0]

            def link(ins):
                chain[0] += 1
                ins.then_inc(sem("vec_chain"), 1)
                dve.wait_ge(sem("vec_chain"), chain[0])

            def tile(name):
                dve.wait_ge(sem("tile_done"), TILE_AT[name] + 1)
                return ps[TILE_AT[name] % BANKS]

            def emptied_by(ins, name):
                assert TURN[name] == turns[0] + 1, name
                turns[0] += 1
                ins.then_inc(sem("emptied_V"), 1)

            def section(name):
                _, row, bias, gain, _ = SECTION[name]
                for j in range(2):
                    cut = slice(j * 512, (j + 1) * 512)
                    if j == 0:
                        dve.wait_ge(sem(f"{name}_bias_in"), 16 if gain is None else 32)
                    o = tile(f"{name}{j}")
                    ins = v.tensor_tensor(row[:, cut], o[0:2, :], bias[:, cut], ALU.add)
                    emptied_by(ins, f"{name}{j}")
                    dve.wait_ge(sem("emptied_V"), turns[0])
                    if gain is not None:
                        v.scalar_tensor_tensor(row[:, cut], row[:, cut], 1.0, gain[:, cut], ALU.add, ALU.mult).then_inc(sem(f"{name}_row"), 1)

            dve.wait_ge(sem("decay_in"), 32)
            link(v.tensor_scalar(s8[:, 1, :], dec, -1.0, None, ALU.mult))
            v.tensor_tensor(s8[:, 0, :], dec, s8[:, 1, :], ALU.max).then_inc(sem("dec_abs"), 1)
            dve.wait_ge(sem("dec_exp"), 1)
            v.tensor_scalar(s8[:, 2, :], s8[:, 1, :], 1.0, None, ALU.add).then_inc(sem("dec_u"), 1)
            dve.wait_ge(sem("dec_u"), 1)
            link(v.tensor_scalar(s8[:, 4, :], s8[:, 2, :], -1.0, None, ALU.add))
            link(v.tensor_scalar(s8[:, 5, :], s8[:, 4, :], 0.0, None, ALU.is_equal))
            link(v.tensor_tensor(s8[:, 4, :], s8[:, 4, :], s8[:, 5, :], ALU.add))
            link(v.reciprocal(s8[:, 6, :], s8[:, 4, :]))
            link(v.tensor_tensor(s8[:, 5, :], s8[:, 5, :], s8[:, 1, :], ALU.mult))
            dve.wait_ge(sem("dec_ln"), 1)
            link(v.tensor_tensor(s8[:, 7, :], s8[:, 3, :], s8[:, 1, :], ALU.mult))
            link(v.tensor_tensor(s8[:, 7, :], s8[:, 7, :], s8[:, 6, :], ALU.mult))
            link(v.tensor_tensor(s8[:, 7, :], s8[:, 7, :], s8[:, 5, :], ALU.add))
            link(v.tensor_scalar(s8[:, 8, :], dec, 0.0, None, ALU.min))
            link(v.tensor_tensor(lg, s8[:, 8, :], s8[:, 7, :], ALU.subtract))
            dve.wait_ge(sem("consts_in"), 16)
            dve.wait_ge(sem("dist_in"), 16)
            for h in range(H):
                link(v.tensor_scalar(DT[:, h, :], dist[:, 0:3 * P], lg[:, h:h + 1], None, ALU.mult))
                link(v.scalar_tensor_tensor(DT[:, h, :], dist[:, 3 * P:6 * P], lg[:, H + h:H + h + 1], DT[:, h, :], ALU.mult, ALU.add))
            for c in range(6):
                d = 0 if c in (0, 1, 4) else H
                ins = v.tensor_scalar(pw[:, c, :], lg[:, d:d + H], cols[:, c:c + 1], None, ALU.mult)
                if c < 5:
                    link(ins)
            ins.then_inc(sem("dec_args"), 1)
            v.tensor_copy(cbf[:, 0, :], const("before")).then_inc(sem("cbf_ready"), 1)
            v.memset(cbf[:, 1, :], 1.0).then_inc(sem("cbf_ready"), 1)
            v.tensor_copy(cbf[:, 2, :], cols[:, 8:9].broadcast_to([P, P])).then_inc(sem("cbf_ready"), 1)

            dve.wait_ge(sem("ssq1"), TT)
            v.tensor_scalar(rstd, ssq, 1.0 / D, EPS, ALU.mult, ALU.add).then_inc(sem("var1"), 1)
            dve.wait_ge(sem("std1"), 1)
            link(v.reciprocal(rstd, rstd))

            def modulate(n, scale, shift):
                rs, rh = SECTION[scale][4], SECTION[shift][4]
                for t in range(TT):
                    c = 0 if t == 0 else 1
                    link(v.scalar_tensor_tensor(work[:, :], x[:, t, :], rstd[:, t:t + 1], rs[:, c, :], ALU.mult, ALU.mult))
                    v.tensor_tensor(HN[n][t].rearrange("p (k q) -> p k q", k=KC), work[:, :].rearrange("p (q k) -> p k q", k=KC),
                                    rh[:, c, :].rearrange("p (q k) -> p k q", k=KC), ALU.add).then_inc(sem(f"h{n}_ready"), 1)
                    dve.wait_ge(sem(f"h{n}_ready"), t + 1)

            def hT_half(n):
                for t in range(TT):
                    name = f"h{n}T{t}1"
                    o = tile(name)
                    ins = v.tensor_copy(hT[:, 4:8, t * P:(t + 1) * P], o[:, :].rearrange("p (k t) -> p k t", k=4))
                    emptied_by(ins, name)

            section("sc1")
            section("sh1")
            dve.wait_ge(sem("emptied_A"), TURN["sh1_row11"])
            modulate(1, "sc1", "sh1")
            hT_half(1)
            dve.wait_ge(sem("pads_written"), 32)
            for g in range(G):
                a = AB[:, g % 2, :]
                if g >= 2:
                    dve.wait_ge(sem("tile_done"), TILE_AT[f"pos{g - 2}"] + 1)
                o = tile(f"chan{g}a")
                emptied_by(v.tensor_copy(a[:, 0:512], o[:, :]), f"chan{g}a")
                o = tile(f"chan{g}b")
                emptied_by(v.tensor_copy(a[:, 512:768], o[:, 0:256]), f"chan{g}b")
            for name, nat in (("q", q_nat), ("k", k_nat)):
                for t in range(TT):
                    o = tile(f"{name}{t}")
                    if t == 0:
                        emptied_by(v.tensor_copy(nat[:, 0, :], o[:, :]), f"{name}{t}")
                        continue
                    cos = const("rope_cos")[:, (t - 1) * P:t * P]
                    sin = const("rope_sin")[:, (t - 1) * P:t * P]
                    cosb = cos.unsqueeze(1).broadcast_to([P, H, P])
                    sin4 = sin.rearrange("p (a b f) -> p a b f", a=2, b=2)
                    src = o[:, :].rearrange("p (h a b f) -> p h a b f", h=H, a=2, b=2)
                    dst = work[:, 0:512].rearrange("p (h a b f) -> p h a b f", h=H, a=2, b=2)
                    for s in range(2):
                        link(v.tensor_tensor(dst[:, :, :, s, :], src[:, :, :, 1 - s, :],
                                             sin4[:, :, s, :].unsqueeze(1).broadcast_to([P, H, 2, 32]), ALU.mult))
                    ins = v.tensor_tensor(work[:, 512:1024].rearrange("p (h n) -> p h n", h=H), o[:, :].rearrange("p (h n) -> p h n", h=H), cosb, ALU.mult)
                    emptied_by(ins, f"{name}{t}")
                    dve.wait_ge(sem("emptied_V"), turns[0])
                    v.tensor_tensor(nat[:, t, :], work[:, 0:512], work[:, 512:1024], ALU.add).then_inc(sem(f"{name}_rotated"), 1)
                    dve.wait_ge(sem(f"{name}_rotated"), t)
            dve.wait_ge(sem("decays"), 2)
            for t in range(TT):
                o = tile(f"kT{t}")
                emptied_by(v.tensor_copy(kT[:, :, t * P:(t + 1) * P], o[:, :].rearrange("p (h t) -> p h t", h=H)), f"kT{t}")
            for d in range(2):
                v.tensor_tensor(kw[:, d, :].rearrange("p (h n) -> p h n", h=H), k_nat[:, 0, :].rearrange("p (h n) -> p h n", h=H),
                                pw[:, 4 + d, :].unsqueeze(2).broadcast_to([P, H, P]), ALU.mult).then_inc(sem("kw_ready"), 1)
            dve.wait_ge(sem("kw_ready"), 2)
            o = tile("sc_ctx")
            emptied_by(v.tensor_tensor(sc_sb[:, 4, :].rearrange("p (h n) -> p h n", h=H), o[:, :].rearrange("p (h n) -> p h n", h=H),
                                       DT[:, :, P:2 * P], ALU.mult), "sc_ctx")
            for h in range(H):
                o = tile(f"sc_lat{h}")
                link(v.tensor_tensor(sc_sb[:, h, 0:LAT], o[:, 0:LAT], DT[:, h, P:3 * P], ALU.mult))
                emptied_by(v.tensor_tensor(sc_sb[:, h, LAT:2 * LAT], o[:, LAT:2 * LAT], DT[:, h, 0:2 * P], ALU.mult), f"sc_lat{h}")
            hn = lambda a: a.rearrange("p (h n) -> p h n", h=H)
            spread4 = lambda a: a.unsqueeze(2).broadcast_to([P, H, P])
            for t in range(TT):
                ow, sq = work[:, 0:512], work[:, 512:1024]
                o = tile(f"o{t}")
                emptied_by(v.tensor_copy(ow, o[:, :]), f"o{t}")
                dve.wait_ge(sem("emptied_V"), turns[0])
                if t:
                    for d, name in ((0, "cross_f"), (1, "cross_b")):
                        o = tile(f"{name}{t}")
                        ins = v.tensor_tensor(hn(sq), hn(o[:, :]), spread4(pw[:, 2 * d + t - 1, :]), ALU.mult)
                        emptied_by(ins, f"{name}{t}")
                        dve.wait_ge(sem("emptied_V"), turns[0])
                        link(v.tensor_tensor(ow, ow, sq, ALU.add))
                mean, var, rs = hst[:, 3 * t, :], hst[:, 3 * t + 1, :], hst[:, 3 * t + 2, :]
                link(v.tensor_reduce(mean, hn(ow), AX.X, ALU.add))
                link(v.tensor_scalar(mean, mean, 1.0 / P, None, ALU.mult))
                link(v.tensor_tensor(hn(ow), hn(ow), spread4(mean), ALU.subtract))
                link(v.tensor_tensor(sq, ow, ow, ALU.mult))
                link(v.tensor_reduce(var, hn(sq), AX.X, ALU.add))
                v.tensor_scalar(var, var, 1.0 / P, EPS, ALU.mult, ALU.add).then_inc(sem("head_var"), 1)
                dve.wait_ge(sem("head_std"), t + 1)
                link(v.reciprocal(rs, var))
                link(v.tensor_tensor(hn(ow), hn(ow), spread4(rs), ALU.mult))
                if t == 0:
                    emptied(dve, "sw2")
                v.tensor_tensor(g_nat[:, t, :], g_nat[:, t, :], ow, ALU.mult).then_inc(sem("ret_ready"), 1)
                dve.wait_ge(sem("ret_ready"), t + 1)
            dve.wait_ge(sem("gn_in"), 16)
            for t in range(TT):
                o = tile(f"retT{t}")
                emptied_by(v.tensor_tensor(retT[:, :, t * P:(t + 1) * P], hn(o[:, :]), spread4(gn_col), ALU.mult), f"retT{t}")
            for m in range(KC):
                o = tile(f"fo{m}")
                dve.wait_ge(sem("emptied_A"), TURN[f"gf{m}"])
                ins = v.tensor_tensor(mergedT[:, m, :], o[:, 0:T], tmpg[:, m % 2, :], ALU.mult)
                emptied_by(ins, f"fo{m}")
            for m in range(KC):
                o = tile(f"ro{m}")
                dve.wait_ge(sem("emptied_A"), TURN[f"gr{m}"])
                ins = v.tensor_tensor(work[:, 0:T], o[:, 0:T], tmpg[:, m % 2, :], ALU.mult)
                emptied_by(ins, f"ro{m}")
                dve.wait_ge(sem("emptied_V"), turns[0])
                v.tensor_tensor(mergedT[:, m, :], mergedT[:, m, :], work[:, 0:T], ALU.add).then_inc(sem("merged"), 1)
                dve.wait_ge(sem("merged"), m + 1)
            section("g1")
            dve.wait_ge(sem("emptied_A"), TURN["g1_row11"])
            for n in range(2):
                for t in range(TT):
                    cut = slice(n * 512, (n + 1) * 512)
                    o = tile(f"mix{n}{t}")
                    ins = v.tensor_tensor(work[:, 0:512], o[:, :], SECTION["g1"][4][:, 0 if t == 0 else 1, cut], ALU.mult)
                    emptied_by(ins, f"mix{n}{t}")
                    dve.wait_ge(sem("emptied_V"), turns[0])
                    ins = v.tensor_tensor(x[:, t, cut], x[:, t, cut], work[:, 0:512], ALU.add)
                    if n:
                        ins.then_inc(sem("x1_ready"), 1)
                        dve.wait_ge(sem("x1_ready"), t + 1)
                    else:
                        link(ins)
            section("sc2")
            section("sh2")
            section("g2")
            dve.wait_ge(sem("ssq2"), TT)
            v.tensor_scalar(rstd, ssq, 1.0 / D, EPS, ALU.mult, ALU.add).then_inc(sem("var2"), 1)
            dve.wait_ge(sem("std2"), 1)
            link(v.reciprocal(rstd, rstd))
            dve.wait_ge(sem("emptied_A"), TURN["g2_row11"])
            modulate(2, "sc2", "sh2")
            hT_half(2)

            dve.wait_ge(sem("emptied_A"), TURN["logits"])
            dve.wait_ge(sem("router_in"), 32)
            for t in range(TT):
                link(v.tensor_tensor(r_bias[:, t, :], r_score[:, t, :], bias_row[:, :], ALU.add))
                m8 = rg[:, 0:64].rearrange("p (g n) -> p g n", g=EG)
                for g in range(EG):
                    link(v.max(m8[:, g, :], r_bias[:, t, g * 8:(g + 1) * 8]))
                gs = rg[:, 64:72]
                link(v.tensor_tensor(gs, m8[:, :, 0], m8[:, :, 1], ALU.add))
                mine = gs.unsqueeze(2).broadcast_to([P, EG, EG])
                other = gs.unsqueeze(1).broadcast_to([P, EG, EG])
                gt = rg[:, 128:192].rearrange("p (a b) -> p a b", a=EG)
                eq = rg[:, 192:256].rearrange("p (a b) -> p a b", a=EG)
                link(v.tensor_tensor(gt, other, mine, ALU.is_gt))
                link(v.tensor_tensor(eq, other, mine, ALU.is_equal))
                link(v.tensor_tensor(eq, eq, const("tie").rearrange("p (a b) -> p a b", a=EG), ALU.mult))
                link(v.tensor_tensor(gt, gt, eq, ALU.add))
                gr = rg[:, 72:80]
                link(v.tensor_reduce(gr, gt, AX.X, ALU.add))
                gm = rg[:, 80:88]
                link(v.tensor_scalar(gm, gr, float(TOPG), None, ALU.is_lt))
                gp = rg[:, 88:96]
                link(v.tensor_scalar(gp, gm, BIG, -BIG, ALU.mult, ALU.add))
                g3 = lambda a: a.rearrange("p (g n) -> p g n", g=EG)
                over8 = lambda a: a.unsqueeze(2).broadcast_to([P, EG, 8])
                link(v.tensor_tensor(g3(r_mask[:, t, :]), g3(r_bias[:, t, :]), over8(gm), ALU.mult))
                link(v.tensor_tensor(g3(r_mask[:, t, :]), g3(r_mask[:, t, :]), over8(gp), ALU.add))
                top = rg[:, 96:104]
                link(v.max(top, r_mask[:, t, :]))
                link(v.match_replace(r_rep[:, t, :], top, r_mask[:, t, :], BIG))
                link(v.tensor_scalar(r_sel[:, t, :], r_rep[:, t, :], BIG, None, ALU.is_equal))
                link(v.tensor_tensor(r_w[:, t, :], r_score[:, t, :], r_sel[:, t, :], ALU.mult))
                ws = rg[:, 104:105]
                link(v.tensor_reduce(ws, r_w[:, t, :], AX.X, ALU.add))
                link(v.reciprocal(rg[:, 105:106], ws))
                link(v.tensor_scalar(r_w[:, t, :], r_w[:, t, :], rg[:, 105:106], ROUTED_SCALE, ALU.mult, ALU.mult))
            v.tensor_copy(sel_bf[:, :, :], r_sel).then_inc(sem("sel_ready"), 1)
            link(v.tensor_copy(M6[:, :, :, 1], cols[:, 8:9].unsqueeze(1).broadcast_to([P, TT, E])))
            link(v.memset(M6[:, :, :, 2], 1.0))
            for t in range(TT):
                link(v.memset(M6[:, t, :, 0], float(P * (t - TT))))
            link(v.tensor_copy(M6[:, :, :, 3], r_w))
            link(v.tensor_tensor(r_x, r_w, M6[:, :, :, 3], ALU.subtract))
            link(v.tensor_copy(M6[:, :, :, 4], r_x))
            link(v.tensor_tensor(r_x, r_x, M6[:, :, :, 4], ALU.subtract))
            v.tensor_copy(M6[:, :, :, 5], r_x).then_inc(sem("m6_ready"), 1)
            for t in range(TT):
                o = tile(f"sgu{t}")
                dve.wait_ge(sem("ssilu_ready"), t + 1)
                ins = v.tensor_tensor(s_hid[t], s_silu, o[:, ED:2 * ED], ALU.mult)
                emptied_by(ins, f"sgu{t}")
            o = tile("rank")
            ins = v.scalar_tensor_tensor(r_rank, o[:, 0:TT * E].rearrange("p (t e) -> p t e", t=TT), 1.0, r_sel, ALU.add, ALU.mult)
            emptied_by(ins, "rank")
            dve.wait_ge(sem("emptied_V"), turns[0])
            link(v.tensor_scalar(r_rank, r_rank, -1.0, None, ALU.add))
            cnt, nb, st, en = [rg[0:E, 256 + n:257 + n] for n in range(4)]
            o = tile("count")
            emptied_by(v.tensor_copy(cnt, o[0:E, 0:1]), "count")
            dve.wait_ge(sem("emptied_V"), turns[0])
            link(v.tensor_scalar(rg[0:E, 264:269], const("over", E), cnt, None, ALU.is_lt))
            link(v.tensor_reduce(nb, rg[0:E, 264:269], AX.X, ALU.add))
            v.tensor_copy(rbf[0:E, 0:1], nb).then_inc(sem("further_ready"), 1)
            o = tile("start")
            emptied_by(v.tensor_copy(st, o[0:E, 0:1]), "start")
            dve.wait_ge(sem("emptied_V"), turns[0])
            link(v.tensor_tensor(en, st, nb, ALU.add))
            slot64 = const("slot", E)
            ge, mine, rnd = rg[0:E, 272:336], rg[0:E, 336:400], rg[0:E, 400:464]
            link(v.tensor_scalar(ge, slot64, st, None, ALU.is_ge))
            link(v.scalar_tensor_tensor(mine, slot64, en, ge, ALU.is_lt, ALU.mult))
            link(v.tensor_scalar(rnd, slot64, st, 1.0, ALU.subtract, ALU.add))
            link(v.tensor_copy(rbf[0:E, MAXOV:2 * MAXOV], mine))
            v.tensor_tensor(rbf[0:E, 2 * MAXOV:3 * MAXOV], rnd, mine, ALU.mult).then_inc(sem("blocks_ready"), 1)
            o = tile("table")
            link(v.tensor_copy(tab[0:1, 0:2 * MAXOV], o[0:1, 0:2 * MAXOV]))
            ins = v.tensor_reduce(rg[0:1, 260:261], o[0:1, 2 * MAXOV:3 * MAXOV:2], AX.X, ALU.add)
            emptied_by(ins, "table")
            dve.wait_ge(sem("emptied_V"), turns[0])
            v.tensor_copy(tab[0:1, 2 * MAXOV:2 * MAXOV + 1], rg[0:1, 260:261]).then_inc(sem("table_ready"), 1)
            for q in range(E // QUAD):
                if q >= 2:
                    dve.wait_ge(sem("onehot_used"), q - 1)
                for t in range(TT):
                    ins = v.tensor_tensor(onehot[:, q % 2, t, :, :],
                                          r_rank[:, t, q * QUAD:(q + 1) * QUAD].unsqueeze(2).broadcast_to([P, QUAD, SLOTS]),
                                          const("slot").unsqueeze(1).broadcast_to([P, QUAD, SLOTS]), ALU.is_equal)
                    if t < TT - 1:
                        link(ins)
                ins.then_inc(sem("onehot_ready"), 1)

            def rows_and_weights(src, at, n, done):
                a, b = work[:, 512:512 + n], work[:, 640:640 + n]
                link(v.tensor_tensor(a, src[:, :, 0], src[:, :, 1], ALU.add))
                link(v.tensor_scalar(b, src[:, :, 2], cols[:, 7:8], cols[:, 6:7], ALU.mult, ALU.add))
                link(v.scalar_tensor_tensor(idx[:, at:at + n], a, 2.0, b, ALU.mult, ALU.add))
                link(v.tensor_tensor(a, src[:, :, 3], src[:, :, 4], ALU.add))
                v.tensor_tensor(cw[:, at:at + n], a, src[:, :, 5], ALU.add).then_inc(sem(done), 1)
                dve.wait_ge(sem(done), 1)

            dve.wait_ge(sem("emptied_A"), TURN["index"])
            rows_and_weights(index_sb, 0, E, "index_ready")
            link(v.memset(slot_ov[:, 0:SLOTS], -7.0))
            for n in range(1, T // SLOTS):
                link(v.tensor_scalar(slot_ov[:, n * SLOTS:(n + 1) * SLOTS], const("slot"), float(n * SLOTS), None, ALU.add))
            dve.wait_ge(sem("h2_written"), 16 * TT)
            link(v.memset(ov_sb, 0.0))
            dve.wait_ge(sem("table_ready"), 1)
            n2 = dve.value_load(tab[0:1, 2 * MAXOV:2 * MAXOV + 1], min_val=0, max_val=MAXOV // 2)
            with dve.If(n2 > 0):
                with dve.Fori(0, n2 * 2) as i:
                    e = dve.value_load(tab[0:1, bass.ds(i, 1)], min_val=0, max_val=E - 1)
                    r = dve.value_load(tab[0:1, bass.ds(i + MAXOV, 1)], min_val=0, max_val=T // SLOTS - 1)
                    for t in range(TT):
                        v.tensor_copy(ov_m6[:, t, :], M6[:, t, bass.ds(e, 1), :].rearrange("p o n -> p (o n)")).then_inc(sem("ov_step"), 1)
                        v.tensor_scalar(onehot[:, 0, t, 0, :], slot_ov[:, bass.ds(r * SLOTS, SLOTS)], r_rank[:, t, bass.ds(e, 1)], None, ALU.is_equal).then_inc(sem("ov_step"), 1)
                    dve.wait_ge(sem("ov_index_done"), i + 1)
                    v.tensor_copy(ov_sb[:, bass.ds(i, 1), :].rearrange("p o n -> p (o n)"), ps[OVB][:, 0:6]).then_inc(sem("ov_copied"), 1)
                    dve.wait_ge(sem("ov_copied"), i + 1)
            dve.nop()
            rows_and_weights(ov_sb, E, MAXOV, "overflow_index_ready")

            def tokens(b, par):
                dve.wait_ge(sem("tokens_used"), b + 1)
                if not (isinstance(b, int) and b < 2):
                    dve.wait_ge(sem("gate_up_done"), b - 1)
                v.tensor_copy(xT[par], ps[4 + par][:, :].rearrange("p (k s) -> p k s", k=4)).then_inc(sem("xT_ready"), 1)

            def hidden(b, par):
                dve.wait_ge(sem("silu_ready"), b + 1)
                if not (isinstance(b, int) and b < 2):
                    dve.wait_ge(sem("hidT_done"), b - 1)
                v.tensor_tensor(hid[par][SLOTS:P, :], sg[par][SLOTS:P, :], ps[par][SLOTS:P, 0:ED], ALU.mult).then_inc(sem("hid_ready"), 1)

            def hidden_T(b, par):
                dve.wait_ge(sem("hidT_done"), b + 1)
                if not (isinstance(b, int) and b < 2):
                    dve.wait_ge(sem("down_done"), b - 1)
                v.tensor_copy(hidT[par], ps[6 + par][:, 0:2 * SLOTS].rearrange("p (j s) -> p j s", j=2)).then_inc(sem("hidT_ready"), 1)

            def step(b, s, more):
                hidden(b, s % 2)
                hidden_T(b, s % 2)
                if more:
                    tokens(b + 1, (s + 1) % 2)

            tokens(0, 0)
            for b in range(NSLOT):
                step(b, b, True)
            with dve.Fori(1, E // NSLOT - 1) as i:
                for s in range(NSLOT):
                    step(i * NSLOT + s, s, True)
            for b in range(E - NSLOT, E):
                step(b, b % NSLOT, b + 1 < E)
            with dve.If(n2 > 0):
                with dve.Fori(0, n2) as i:
                    for s in range(2):
                        b = i * 2 + (E + s)
                        tokens(b, s)
                        hidden(b, s)
                        hidden_T(b, s)
            dve.nop()

            dve.wait_ge(sem("fin_in"), 16)
            yv = hT[:, :, :].rearrange("p k t -> p (k t)")
            for t in range(TT):
                dve.wait_ge(sem(f"y_in{t}"), 16)
                link(v.tensor_tensor(work[:, :], yv[:, t * D:(t + 1) * D], SECTION["g2"][4][:, 0 if t == 0 else 1, :], ALU.mult))
                v.tensor_tensor(x[:, t, :], x[:, t, :], work[:, :], ALU.add).then_inc(sem("x2_ready"), 1)
                dve.wait_ge(sem("x2_ready"), t + 1)
            for t in range(TT):
                dve.wait_ge(sem("ssq3"), t + 1)
                v.tensor_scalar(rstd[:, t:t + 1], ssq[:, t:t + 1], 1.0 / D, EPS, ALU.mult, ALU.add).then_inc(sem("var3"), 1)
                dve.wait_ge(sem("std3"), t + 1)
                link(v.reciprocal(rstd[:, t:t + 1], rstd[:, t:t + 1]))
                v.scalar_tensor_tensor(x[:, t, :], x[:, t, :], rstd[:, t:t + 1], fin_g, ALU.mult, ALU.mult).then_inc(sem("out_ready"), 1)


_INS = ["x_prompt", "x_sample", "state_ret_fwd", "state_ret_bwd", "c", "c_ctx", "w_ada", "b_ada", "norm1_g", "norm2_g",
        "w_in", "ret_decay_fwd", "ret_decay_bwd", "ret_gn_g", "w_four_out", "w_ret_out", "w_out", "w_router",
        "router_bias", "w_exp_gate", "w_exp_up", "w_exp_down", "w_shared_gate", "w_shared_up", "w_shared_down",
        "final_norm_g"]
_OUTS = [(1, CTX, D), (1, LAT, D), (1, 1, H, P, P), (1, 1, H, P, P)]


def kernel(**inputs):
    from concourse import bacc
    from concourse.bass_utils import run_bass_kernel_spmd

    nc = bacc.Bacc("TRN2", target_bir_lowering=False, num_devices=1)
    arrays, args = {}, {}
    for name in _INS:
        a = np.ascontiguousarray(inputs[name])
        arrays[f"in_{name}"] = a
        args[name] = nc.dram_tensor(f"in_{name}", a.shape, mybir.dt.from_np(a.dtype), kind="ExternalInput").ap()
    table = constants()[0]
    arrays["in_consts"] = table
    consts = nc.dram_tensor("in_consts", table.shape, F32, kind="ExternalInput").ap()
    arrays["in_dists"] = distances()
    dists = nc.dram_tensor("in_dists", (P, 6 * P), F32, kind="ExternalInput").ap()
    outs = [nc.dram_tensor(f"out_{i}", shape, F32, kind="ExternalOutput").ap() for i, shape in enumerate(_OUTS)]
    trunk_kernel(nc, args, outs, consts, dists)
    r = run_bass_kernel_spmd(nc, [arrays], core_ids=[0])
    return tuple(r.results[0][f"out_{i}"] for i in range(len(_OUTS)))
```

```python
import numpy as np
import concourse.bass as bass
from concourse import mybir
from concourse.alu_op_type import AluOpType as ALU
from contextlib import ExitStack

F32 = mybir.dt.float32
BF16 = mybir.dt.bfloat16
I32 = mybir.dt.int32
ACT = mybir.ActivationFunctionType
AX = mybir.AxisListType

P = 128
D = 1024
KC = D // P
CTX, LAT = 128, 256
T = CTX + LAT
TT = T // P
H = 4
RW = H * P
G = 8
E = 64
EG = 8
TOPG = 4
ED = 256
SLOTS = 64
EPS = 1e-6
ROUTED_SCALE = 2.5
GRID_W = 64
ROPE_BASE = 10000.0
ROWS = 2 * T + P
BIG = 3.0e38
CELL = 2048
PIECE = 2 * CELL
NPIECE_SLOTS = 6
NSLOT = 4
EXPERT = 3 * CELL
FURTHER = 64
BANKS = 8


def constants():
    a = np.arange
    parts = {}
    parts["ident"] = np.eye(P)
    parts["ident_pair"] = np.tile(np.eye(E), (P // E, 1))
    c = 2 * np.pi * ((a(P)[:, None] * a(P)[None]) % P) / P
    parts["dft_chan"] = np.concatenate([np.cos(c), np.sin(c)], 1)
    n = (CTX * P) ** -0.5
    parts["dft_ctx"] = np.concatenate([np.cos(c) * n, -np.sin(c) * n], 1)
    w = 2 * np.pi * ((a(LAT)[:, None] * a(LAT)[None]) % LAT) / LAT
    n = (LAT * P) ** -0.5
    both = np.stack([np.cos(w) * n, -np.sin(w) * n], 1).reshape(2, P, 2 * LAT)
    parts["dft_lat"] = np.concatenate([both[0], both[1]], 1)
    nf = P // 4
    inv = np.float32(ROPE_BASE) ** (-a(nf, dtype=np.float32) / np.float32(nf))
    t = a(LAT)
    ar = (t // GRID_W).astype(np.float32)[:, None] * inv[None]
    ac = (t % GRID_W).astype(np.float32)[:, None] * inv[None]
    ang = np.concatenate([ar, ar, ac, ac], 1).astype(np.float64)
    sign = np.where((a(P) // nf) % 2 == 0, -1.0, 1.0)
    cos, sin = np.cos(ang), np.sin(ang) * sign
    parts["rope_cos"] = np.concatenate([cos[:P], cos[P:]], 1)
    parts["rope_sin"] = np.concatenate([sin[:P], sin[P:]], 1)
    parts["before"] = (a(P)[:, None] < a(P)[None]).astype(float)
    parts["slot"] = np.tile(a(1, SLOTS + 1)[None], (P, 1))
    nr = T // SLOTS
    parts["tie"] = np.tile((a(EG)[None] < a(EG)[:, None]).astype(float).reshape(1, -1), (P, 1))
    parts["over"] = np.tile((SLOTS * a(1, nr))[None], (P, 1))
    p = a(P)
    cols = [p + 1, p + 1 + P, LAT - p, LAT - P - p, CTX - 1 - p, p,
            2 * T + p, p // SLOTS - p, p, p % 32 == 0, p % 32 == 1]
    parts["cols"] = np.stack([np.asarray(c, float) for c in cols], 1)
    at, out, n = {}, [], 0
    for k, v in parts.items():
        at[k] = (n, n + v.shape[1])
        n += v.shape[1]
        out.append(v.astype(np.float32))
    return np.concatenate(out, 1), at


def distances():
    delta = np.arange(3 * P)[None] - P - np.arange(P)[:, None]
    return np.concatenate([np.maximum(delta, 0), np.maximum(-delta, 0)], 1).astype(np.float32)


CONST_AT = constants()[1]
NCONST = max(b for _, b in CONST_AT.values())

PIECES = (["ada2", "ada3", "ada0", "ada1"] + [f"win{i}" for i in range(6)]
          + ["win6", "four0", "win7", "four1", "win8", "win9", "ret", "ada4", "ada5", "out0", "out1",
             "ada8", "ada9", "ada6", "ada7", "ada10", "ada11", "sgu", "sd"])
PIECE_AT = {name: n for n, name in enumerate(PIECES)}


def psum_tiles():
    out = []

    def mod(name, parts=(0, 1)):
        if 0 in parts:
            out.extend((f"{name}{j}", "V") for j in range(2))
        if 1 in parts:
            out.extend((f"{name}_row{c}{j}", "V" if name.startswith("sc") else "A") for c in range(2) for j in range(2))

    mod("sc1")
    mod("sh1")
    for t in range(TT):
        out.extend([(f"h1T{t}0", "A"), (f"h1T{t}1", "V")])
    out.extend((f"uf{g}", "A") for g in range(G))
    for g in range(G + 1):
        if g < G:
            out.extend([(f"chan{g}a", "V"), (f"chan{g}b", "V")])
        if g > 0:
            out.append((f"pos{g - 1}", "A"))
    for n, eng in (("q", "V"), ("k", "V"), ("v", "A"), ("sw", "A")):
        out.extend((f"{n}{t}", eng) for t in range(TT))
    for t in range(TT):
        out.extend([(f"qT{t}", "A"), (f"kT{t}", "V")])
    out.extend([("state0", "A"), ("state1", "A"), ("sc_ctx", "V")])
    out.extend((f"sc_lat{h}", "V") for h in range(H))
    out.append(("o0", "V"))
    for t in (1, 2):
        out.extend([(f"o{t}", "V"), (f"cross_f{t}", "V"), (f"cross_b{t}", "V")])
    for m in range(KC):
        out.extend([(f"gf{m}", "A"), (f"fo{m}", "V")])
    out.extend((f"retT{t}", "V") for t in range(TT))
    for m in range(KC):
        out.extend([(f"gr{m}", "A"), (f"ro{m}", "V")])
    mod("g1")
    out.extend((f"mix{n}{t}", "V") for n in range(2) for t in range(TT))
    mod("sc2")
    mod("sh2")
    for t in range(TT):
        out.extend([(f"h2T{t}0", "A"), (f"h2T{t}1", "V")])
    mod("g2", (0,))
    out.extend([("logitsT", "A"), ("logits", "A")])
    mod("g2", (1,))
    out.extend([("sgu0", "V"), ("rank", "V"), ("count", "V"), ("sgu1", "V"), ("start", "V"), ("table", "V"),
                ("rankT", "A"), ("wT", "A"), ("rank_x", "V"), ("w_x", "V"), ("sgu2", "V")])
    out.extend((f"shT{t}", "A") for t in range(TT))
    out.extend([("sd00", "V"), ("sd01", "V"), ("index", "A"), ("further", "A")])
    out.extend((f"sd{t}{n}", "V") for t in (1, 2) for n in range(2))
    return out


TILES = psum_tiles()
TILE_AT = {name: n for n, (name, _) in enumerate(TILES)}
TURN = {}
for _n, (_name, _eng) in enumerate(TILES):
    TURN[_name] = sum(e == _eng for _, e in TILES[:_n + 1])
LAST_READ = {f"ada{i}": f"{name}{i % 2}" for name, i0 in (("sh1", 0), ("sc1", 2), ("g1", 4), ("sh2", 6), ("sc2", 8), ("g2", 10))
             for i in (i0, i0 + 1)}
LAST_READ |= {"win0": "uf3", "win1": "uf7", "win2": "q2", "win3": "k2", "win4": "v2", "win5": "sw2", "win6": "gf3",
              "four0": "fo3", "win7": "gf7", "four1": "fo7", "win8": "gr3", "win9": "gr7", "ret": "ro7",
              "out0": "mix02", "out1": "mix12", "sgu": "sgu2", "sd": "sd21"}
QUAD = 16


def trunk_kernel(nc, A, outs, consts, dists):
    y_prompt, y_sample, new_f, new_b = outs
    ctx = ExitStack()
    with ctx:
        def sb(name, shape, dt=F32):
            return ctx.enter_context(nc.sbuf_tensor(name, shape, dt))

        ring = sb("ring", [P, NSLOT * EXPERT])
        C = sb("consts_sb", [P, NCONST])
        x = sb("x", [P, TT, D])
        hT = sb("hT", [P, KC, T])
        U = sb("U", [P, 3072])
        Fm = sb("Fm", [P, 3072])
        VG = sb("VG", [P, 3072])
        QK = sb("QK", [P, 3072])
        DT = sb("DT", [P, H, 3 * P])
        MB = sb("MB", [P, 1024])
        S0 = sb("S0", [P, 2, H, P])
        AB = sb("AB", [P, 2, 768])
        work = sb("work", [P, 1024])
        small = sb("small", [P, 256])
        cond = sb("cond", [P, 2, KC])
        condr = sb("condr", [P, KC, 32])
        cbf = sb("cbf", [P, 2, P], BF16)
        idx = sb("idx", [P, E + FURTHER], I32)
        cw = sb("cw", [P, E + FURTHER])
        gather_rows = sb("gather_rows", [P, NSLOT], I32)
        scatter_rows = sb("scatter_rows", [P, NSLOT], I32)
        rows_further = sb("rows_further", [P, 2], I32)
        tab = sb("tab", [1, 2 * E + 2], I32)
        ps = [ctx.enter_context(nc.psum_tensor(f"bank{i}", [P, 512], F32)) for i in range(BANKS)]
        h2_rows = nc.dram_tensor("h2_rows", [ROWS, 512], F32, kind="Internal").ap()
        y_rows = [nc.dram_tensor(f"y_rows{n}", [ROWS, 512], F32, kind="Internal").ap() for n in range(3)]

        sems = {}

        def sem(name):
            if name not in sems:
                sems[name] = ctx.enter_context(nc.semaphore(name))
            return sems[name]

        def const(name, rows=P):
            a, b = CONST_AT[name]
            return C[0:rows, a:b]

        ident = const("ident")
        cols = const("cols")

        uT = U[:, :].rearrange("p (g t) -> p g t", g=G)
        q_nat = U[:, 0:1536].rearrange("p (t n) -> p t n", t=TT)
        k_nat = U[:, 1536:3072].rearrange("p (t n) -> p t n", t=TT)
        sc_sb = U[:, 0:2560].rearrange("p (h n) -> p h n", h=5)
        mergedT = uT
        fmixT = Fm[:, :].rearrange("p (g t) -> p g t", g=G)
        v_nat = VG[:, 0:1536].rearrange("p (t n) -> p t n", t=TT)
        g_nat = VG[:, 1536:3072].rearrange("p (t n) -> p t n", t=TT)
        qT = QK[:, 0:1536].rearrange("p (h t) -> p h t", h=H)
        kT = QK[:, 1536:3072].rearrange("p (h t) -> p h t", h=H)
        retT = qT
        kw = AB[:, :, 0:512]
        lg = small[:, 0:8]
        pw = small[:, 8:32].rearrange("p (c h) -> p c h", c=6)
        ssq = small[:, 32:35]
        rstd = small[:, 35:38]
        dec = small[:, 40:48]
        gn_col = small[:, 48:52]
        s8 = small[:, 56:136].rearrange("p (n c) -> p n c", c=8)
        hst = small[:, 136:184].rearrange("p (n c) -> p n c", c=4)
        AB1 = AB[:, :, :].rearrange("p a b -> p (a b)")

        def rows_of(buf, at):
            return buf[:, at:at + 2048].rearrange("p (c n) -> p c n", c=2)

        DTf = DT[:, :, :].rearrange("p h n -> p (h n)")
        S0f = S0[:, :, :, :].rearrange("p a h e -> p (a h e)")
        wr = DTf[:, 1024:1536].rearrange("p (k e) -> p k e", k=KC)
        dist = MB[:, 0:768]
        tmpg = S0f[:, 0:2 * T].rearrange("p (b t) -> p b t", b=2)
        M6 = S0f[:, :].bitcast(BF16)[:, 0:TT * E * 6].rearrange("p (t e n) -> p t e n", t=TT, e=E)
        state_sb = MB[:, :].rearrange("p (d h e) -> p d h e", d=2, h=H)
        shT_sb = MB[:, 0:768].rearrange("p (t j q) -> p t j q", t=TT, j=2)
        junk = {1: VG[:, 2048:3072], 2: VG[:, 2048:3072], 3: QK[:, 0:1024]}
        SECTION = {
            "sc1": (2, QK[:, 0:1024], QK[0:2, 1024:2048], QK[:, 2048:3072], rows_of(Fm, 0)),
            "sh1": (0, U[:, 0:1024], U[0:2, 1024:2048], None, rows_of(VG, 0)),
            "g1": (4, AB1[:, 0:1024], VG[0:2, 2048:3072], None, rows_of(VG, 0)),
            "sc2": (8, AB1[:, 0:1024], QK[0:2, 2048:3072], Fm[:, 2048:3072], rows_of(Fm, 0)),
            "sh2": (6, U[:, 2048:3072], DTf[0:2, 0:1024], None, rows_of(QK, 0)),
            "g2": (10, S0f[:, :], AB1[0:2, 0:1024], None, rows_of(U, 0)),
        }
        HN = {1: [Fm[:, 2048:3072], VG[:, 2048:3072], U[:, 2048:3072]],
              2: [VG[:, 0:1024], VG[:, 1024:2048], VG[:, 2048:3072]]}

        onehot = Fm[:, :].bitcast(BF16).rearrange("p (b c e s) -> p b c e s", b=2, c=TT, e=QUAD)
        hTf = hT[:, :, :].rearrange("p k t -> p (k t)")
        xg = [QK[:, 0:512], QK[:, 512:1024], hTf[:, 0:512], hTf[:, 512:1024]]
        xT = [QK[:, 1024:1536].rearrange("p (k s) -> p k s", k=4), QK[:, 1536:2048].rearrange("p (k s) -> p k s", k=4)]
        sg = [VG[:, 0:256], VG[:, 256:512]]
        hid = [VG[:, 512:768], VG[:, 768:1024]]
        hidT = [VG[:, 1024:1152].rearrange("p (j s) -> p j s", j=2), VG[:, 1152:1280].rearrange("p (j s) -> p j s", j=2)]
        yb = [VG[:, 1280:1792], VG[:, 1792:2304], hTf[:, 1024:1536], hTf[:, 1536:2048]]
        index_sb = VG[:, 2304:2688].rearrange("p (e n) -> p e n", n=6)
        further_sb = VG[:, 2688:3072].rearrange("p (e n) -> p e n", n=6)
        xg_f = QK[:, 2048:2560]
        xT_f = QK[:, 2560:3072].rearrange("p (k s) -> p k s", k=4)
        sg_f, hid_f = U[:, 2048:2304], U[:, 2304:2560]
        hidT_f = U[:, 2560:2688].rearrange("p (j s) -> p j s", j=2)
        yb_f = AB1[:, 1024:1536]
        s_silu = AB1[:, 0:256]
        s_hid = [AB1[:, 256:512], AB1[:, 512:768], AB1[:, 768:1024]]
        fin_g = AB1[:, 0:1024]
        R = DTf.rearrange("p (n c e) -> p n c e", n=8, c=TT)
        r_score, r_bias, r_mask, r_rep, r_sel, r_w, r_rank, r_x = [R[:, n, :, :] for n in range(8)]
        further_bf = sb("further_bf", [E, 1], BF16)
        M6X = DTf.bitcast(BF16)[:, 2 * TT * E:2 * TT * E + TT * FURTHER * 6].rearrange("p (t e n) -> p t e n", t=TT, e=FURTHER)
        rankT = U[0:E, 2048:2048 + T]
        wT = U[0:E, 2048 + T:2048 + 2 * T]
        minus_slots = U[0:E, 2048 + 2 * T:2048 + 2 * T + P]
        rank_x = AB1[:, 1024:1216].rearrange("p (t e) -> p t e", t=TT)
        logitsT = AB1[:, 1024:1024 + T]
        w_x = AB1[:, 1216:1408].rearrange("p (t e) -> p t e", t=TT)
        sel_bf = sb("sel_bf", [P, TT, E], BF16)
        bias_row = sb("bias_row", [P, E])
        rg = work[:, :]
        further_n, before_n, end_n, total = [rg[0:E, n:n + 1] for n in (257, 258, 259, 260)]
        total = total[0:1, :]
        since, mine, rounds = rg[0:E, 272:336], rg[0:E, 336:400], rg[0:E, 400:464]

        w_ada = A["w_ada"].rearrange("o (p k) n -> (o p) k n", p=P)
        w_in = A["w_in"].rearrange("o (p k) n -> (o p) k n", p=P)
        w_four = A["w_four_out"].rearrange("o (k p) n -> (o p) k n", p=P)
        w_out = A["w_out"].rearrange("o (k p) n -> (o p) k n", p=P)
        w_ret = A["w_ret_out"].rearrange("o (k p) n -> (o p) k n", p=P)
        w_sg = A["w_shared_gate"].rearrange("o (p k) n -> (o p) k n", p=P)
        w_su = A["w_shared_up"].rearrange("o (p k) n -> (o p) k n", p=P)
        w_sd = A["w_shared_down"].rearrange("o (p k) n -> (o p) k n", p=P)
        w_eg = A["w_exp_gate"].rearrange("o e (p k) f -> (o e p) (k f)", p=P)
        w_eu = A["w_exp_up"].rearrange("o e (p k) f -> (o e p) (k f)", p=P)
        w_ed = A["w_exp_down"].rearrange("o e (p j) d -> (o e p) (j d)", p=P)
        b_ada = A["b_ada"]

        def piece(name):
            s = PIECE_AT[name] % NPIECE_SLOTS
            return ring[:, s * PIECE:(s + 1) * PIECE]

        def piece_landed(eng, name):
            n = PIECE_AT[name]
            eng.wait_ge(sem(f"piece_slot{n % NPIECE_SLOTS}"), LANDED[name])

        LANDED, at = {}, [0] * NPIECE_SLOTS
        for n, name in enumerate(PIECES):
            at[n % NPIECE_SLOTS] += 32 if name == "sgu" else 16
            LANDED[name] = at[n % NPIECE_SLOTS]

        def expert(s):
            w = ring[:, s * EXPERT:(s + 1) * EXPERT]
            return (w[:, 0:CELL].rearrange("p (k f) -> p k f", k=KC),
                    w[:, CELL:2 * CELL].rearrange("p (k f) -> p k f", k=KC),
                    w[:, 2 * CELL:3 * CELL].rearrange("p (j d) -> p j d", j=2))

        def emptied(eng, name):
            eng.wait_ge(sem(f"emptied_{TILES[TILE_AT[name]][1]}"), TURN[name])

        def computed(eng, name):
            eng.wait_ge(sem("tile_done"), TILE_AT[name] + 1)

        for name in ("tile_done", "emptied_A", "emptied_V"):
            sem(name)

        block = ctx.enter_context(nc.Block())

        def stand_alone(eng, signal):
            eng.sem_inc(sem(signal), 1)

        def column(table, b):
            return table[:, b:b + 1] if isinstance(b, int) else table[:, bass.ds(b, 1)]

        def many(eng):
            eng.wait_ge(sem("table_ready"), 1)
            return eng.value_load(tab[0:1, 2 * E:2 * E + 1], min_val=0, max_val=1)

        def further_blocks(eng, e, block):
            n = eng.value_load(column(tab[0:1, :], e), min_val=0, max_val=T // SLOTS - 1)
            with eng.If(n > 0):
                first = eng.value_load(column(tab[0:1, :], e + E), min_val=0, max_val=FURTHER - T // SLOTS)
                with eng.Fori(0, n) as i:
                    block(first + i)

        def bias_rows(eng, name):
            i, _, bias, gain, _ = SECTION[name]
            eng.dma_start(bias, b_ada[0:1, i * 512:i * 512 + D].broadcast_to([2, D])).then_inc(sem(f"{name}_bias_in"), 16)
            if gain is not None:
                g = A["norm1_g"] if name == "sc1" else A["norm2_g"]
                eng.dma_start(gain, g[0:1, :].broadcast_to([P, D])).then_inc(sem(f"{name}_bias_in"), 16)

        def load_expert(sp, row, s):
            w = ring[:, s * EXPERT:(s + 1) * EXPERT]
            src = (lambda a: a[row:row + P, :]) if isinstance(row, int) else (lambda a: a[bass.ds(row, P), :])
            sp.dma_start(w[:, 0:CELL], src(w_eg)).then_inc(sem(f"gate_up_slot{s}"), 16)
            sp.dma_start(w[:, CELL:2 * CELL], src(w_eu)).then_inc(sem(f"gate_up_slot{s}"), 16)
            sp.dma_start(w[:, 2 * CELL:3 * CELL], src(w_ed)).then_inc(sem(f"down_slot{s}"), 16)

        @block.sync
        def _(sp):
            sp.dma_start(cond[:, 0, :], A["c_ctx"].rearrange("(p k) -> p k", p=P)).then_inc(sem("cond_in"), 16)
            sp.dma_start(cond[:, 1, :], A["c"].rearrange("o (p k) -> (o p) k", p=P)).then_inc(sem("cond_in"), 16)
            for n, name in enumerate(PIECES):
                if name == "ada3":
                    bias_rows(sp, "sc1")
                elif name == "ada0":
                    sp.dma_start(C[:, :], consts).then_inc(sem("consts_in"), 16)
                    sp.dma_start(x[:, 0, :], A["x_prompt"][0, :, :]).then_inc(sem("x_in"), 16)
                    sp.dma_start(x[:, 1:3, :], A["x_sample"][0, :, :].rearrange("(t p) d -> p t d", p=P)).then_inc(sem("x_in"), 16)
                elif name == "win0":
                    bias_rows(sp, "sh1")
                dst = piece(name).rearrange("p (k n) -> p k n", k=KC)
                if n >= NPIECE_SLOTS:
                    computed(sp, LAST_READ[PIECES[n - NPIECE_SLOTS]])
                landed = sem(f"piece_slot{n % NPIECE_SLOTS}")
                if name.startswith("ada"):
                    i = int(name[3:])
                    sp.dma_start(dst, w_ada[:, :, i * 512:(i + 1) * 512]).then_inc(landed, 16)
                elif name.startswith("win"):
                    i = int(name[3:])
                    sp.dma_start(dst, w_in[:, :, i * 512:(i + 1) * 512]).then_inc(landed, 16)
                elif name.startswith("four"):
                    i = int(name[4:])
                    sp.dma_start(dst, w_four[:, :, i * 512:(i + 1) * 512]).then_inc(landed, 16)
                elif name.startswith("out"):
                    i = int(name[3:])
                    sp.dma_start(dst, w_out[:, :, i * 512:(i + 1) * 512]).then_inc(landed, 16)
                elif name == "ret":
                    sp.dma_start(piece(name).rearrange("p (k n) -> p k n", k=H), w_ret).then_inc(landed, 16)
                elif name == "sgu":
                    sp.dma_start(dst[:, :, 0:ED], w_sg).then_inc(landed, 16)
                    sp.dma_start(dst[:, :, ED:2 * ED], w_su).then_inc(landed, 16)
                else:
                    sp.dma_start(piece(name)[:, 0:CELL].rearrange("p (k n) -> p k n", k=2), w_sd).then_inc(landed, 16)
            last = len(PIECES)
            for s in range(NSLOT):
                lo, hi = s * EXPERT // PIECE, ((s + 1) * EXPERT - 1) // PIECE
                need = max(n for n in range(last) if lo <= n % NPIECE_SLOTS <= hi)
                computed(sp, LAST_READ[PIECES[need]])
                load_expert(sp, s * P, s)
            with sp.Fori(1, E // NSLOT) as i:
                for s in range(NSLOT):
                    sp.wait_ge(sem("down_done"), i * NSLOT + (s - NSLOT + 1))
                    load_expert(sp, i * (NSLOT * P) + s * P, s)
            for n in range(2):
                sp.wait_ge(sem(f"scattered{n}"), 8 * E)
            for t in range(TT):
                for n, dst in enumerate((hTf, VG)):
                    sp.dma_start(dst[:, t * D:(t + 1) * D],
                                 y_rows[n][2 * t * P:2 * (t + 1) * P, :].rearrange("(p j) n -> p (j n)", j=2)).then_inc(sem(f"y_in{t}"), 16)
            for t in range(TT):
                sp.wait_ge(sem("out_ready"), t + 1)
                dst = y_prompt[0, :, :] if t == 0 else y_sample[0, (t - 1) * P:t * P, :]
                sp.dma_start(dst, x[:, t, :]).then_inc(sem("out_written"), 16)
            sp.wait_ge(sem("out_written"), 16 * TT)

        def gather(pool, b, s):
            nc.gpsimd.tensor_copy(gather_rows[:, s:s + 1], column(idx, b)).then_inc(sem("gather_rows_ready"), 1)
            pool.wait_ge(sem("gather_rows_ready"), b + 1)
            stand_alone(pool, "pool_passed")
            pool.indirect_dma_start(xg[s], None, h2_rows, bass.IndirectOffsetOnAxis(gather_rows[:, s:s + 1], 0),
                                    bounds_check=ROWS - 1).then_inc(sem(f"gathered{s}"), 16)

        def scatter_add(pool, b, s):
            nc.gpsimd.tensor_copy(scatter_rows[:, s:s + 1], column(idx, b)).then_inc(sem("scatter_rows_ready"), 1)
            pool.wait_ge(sem("scatter_rows_ready"), b + 1)
            pool.wait_ge(sem("y_ready"), b + 1)
            if not (isinstance(b, int) and b < 2):
                pool.wait_ge(sem(f"scattered{s % 2}"), (b - s % 2) * 8)
            stand_alone(pool, "pool_passed")
            pool.indirect_dma_start(y_rows[s % 2], bass.IndirectOffsetOnAxis(scatter_rows[:, s:s + 1], 0), yb[s], None,
                                    bounds_check=ROWS - 1, compute_op=ALU.add).then_inc(sem(f"scattered{s % 2}"), 16)

        @block.gpsimd
        def _(pool):
            pool.dma_start(dist, dists).then_inc(sem("dist_in"), 16)
            pool.dma_start(dec[:, 0:4], A["ret_decay_fwd"][0:1, :].broadcast_to([P, H])).then_inc(sem("decay_in"), 16)
            pool.dma_start(dec[:, 4:8], A["ret_decay_bwd"][0:1, :].broadcast_to([P, H])).then_inc(sem("decay_in"), 16)
            pool.dma_start(S0[:, 0, :, :], A["state_ret_fwd"][0, 0].rearrange("h d e -> d h e")).then_inc(sem("state_in"), 16)
            pool.dma_start(S0[:, 1, :, :], A["state_ret_bwd"][0, 0].rearrange("h d e -> d h e")).then_inc(sem("state_in"), 16)
            pool.dma_start(gn_col, A["ret_gn_g"].rearrange("o (h p) -> (o p) h", p=P), allow_slow_non_contiguous=True).then_inc(sem("gn_in"), 16)
            pool.dma_start(bias_row[:, :], A["router_bias"][0:1, :].broadcast_to([P, E])).then_inc(sem("router_in"), 16)
            computed(pool, "uf3")
            nc.gpsimd.memset(QK[:, 0:512], 0.0).then_inc(sem("zeros"), 1)
            pool.wait_ge(sem("zeros"), 1)
            pool.dma_start(h2_rows[2 * T:ROWS, :], QK[:, 0:512]).then_inc(sem("pads_written"), 16)
            for n in range(3):
                pool.dma_start(y_rows[n].rearrange("(n p) c -> p n c", p=P),
                               QK[:, 0:512].unsqueeze(1).broadcast_to([P, ROWS // P, 512])).then_inc(sem("pads_written" if n < 2 else "f_scattered"), 16)
            pool.wait_ge(sem("pads_written"), 48)
            pool.wait_ge(sem("f_scattered"), 16)

            emptied(pool, "state1")
            pool.dma_start(new_f[0, 0].rearrange("h d e -> d h e"), state_sb[:, 0, :, :]).then_inc(sem("states_written"), 16)
            pool.dma_start(new_b[0, 0].rearrange("h d e -> d h e"), state_sb[:, 1, :, :]).then_inc(sem("states_written"), 16)
            pool.wait_ge(sem("states_written"), 32)
            computed(pool, "retT2")
            bias_rows(pool, "g1")
            computed(pool, "ro7")
            pool.dma_start(wr, A["w_router"].rearrange("o (p k) e -> (o p) k e", p=P)).then_inc(sem("router_in"), 16)
            bias_rows(pool, "sc2")
            bias_rows(pool, "sh2")
            computed(pool, "sc2_row11")
            bias_rows(pool, "g2")
            for t in range(TT):
                pool.wait_ge(sem("h2_ready"), t + 1)
                pool.dma_start(h2_rows[2 * t * P:2 * (t + 1) * P, :].rearrange("(p j) n -> p (j n)", j=2),
                               HN[2][t]).then_inc(sem("h2_written"), 16)
            computed(pool, "shT2")
            pool.dma_start(fin_g, A["final_norm_g"].rearrange("(o n) -> o n", o=1).broadcast_to([P, D])).then_inc(sem("fin_in"), 16)
            pool.wait_ge(sem("h2_written"), 16 * TT)

            pool.wait_ge(sem("index_ready"), 5)
            for b in range(NSLOT):
                if b == 2:
                    computed(pool, "sgu2")
                gather(pool, b, b)
            pool.wait_ge(sem("further_index_ready"), 1)
            pool.wait_ge(sem("table_ready"), 1)

            def gather_further(u):
                nc.gpsimd.tensor_copy(rows_further[:, 0:1], column(idx, u + E)).then_inc(sem("f_gather_ready"), 1)
                pool.wait_ge(sem("f_gather_ready"), u + 1)
                stand_alone(pool, "pool_passed")
                pool.indirect_dma_start(xg_f, None, h2_rows, bass.IndirectOffsetOnAxis(rows_further[:, 0:1], 0),
                                        bounds_check=ROWS - 1).then_inc(sem("f_gathered"), 16)

            def further(e):
                def block(u):
                    pool.wait_ge(sem("f_tokens_used"), u + 1)
                    stand_alone(pool, "pool_passed")
                    gather_further(u + 1)
                    pool.wait_ge(sem("f_scattered"), u * 16 + 16)
                    stand_alone(pool, "pool_passed")
                    nc.gpsimd.tensor_copy(rows_further[:, 1:2], column(idx, u + E)).then_inc(sem("rows_further_ready"), 1)
                    pool.wait_ge(sem("rows_further_ready"), u + 1)
                    pool.wait_ge(sem("f_y_ready"), u + 1)
                    stand_alone(pool, "pool_passed")
                    pool.indirect_dma_start(y_rows[2], bass.IndirectOffsetOnAxis(rows_further[:, 1:2], 0), yb_f, None,
                                            bounds_check=ROWS - 1, compute_op=ALU.add).then_inc(sem("f_scattered"), 16)
                further_blocks(pool, e, block)

            def step(b, s):
                if not (isinstance(b, int) and b + NSLOT >= E):
                    pool.wait_ge(sem("tokens_used"), b + 1)
                    stand_alone(pool, "pool_passed")
                    gather(pool, b + NSLOT, s)
                if not (isinstance(b, int) and b + 1 >= E):
                    further(b + 1)
                scatter_add(pool, b, s)

            gather_further(0)
            further(0)
            for b in range(NSLOT):
                step(b, b)
            with pool.Fori(1, E // NSLOT - 1) as i:
                for s in range(NSLOT):
                    step(i * NSLOT + s, s)
            for b in range(E - NSLOT, E - 1):
                step(b, b % NSLOT)
            total = pool.value_load(tab[0:1, 2 * E + 1:2 * E + 2], min_val=0, max_val=FURTHER - T // SLOTS)
            pool.wait_ge(sem("f_gathered"), total * 16 + 16)
            pool.wait_ge(sem("f_scattered"), total * 16 + 16)
            stand_alone(pool, "pool_passed")
            pool.dma_start(Fm[:, :].rearrange("p (t n) -> p t n", t=TT),
                           y_rows[2][0:2 * T, :].rearrange("(t p j) n -> p t (j n)", t=TT, j=2)).then_inc(sem("y2_in"), 16)
            scatter_add(pool, E - 1, (E - 1) % NSLOT)
            for t in (1, 2):
                pool.wait_ge(sem(f"y_in{t}"), 32)
                cut = slice(t * D, (t + 1) * D)
                nc.gpsimd.tensor_tensor(hTf[:, cut], hTf[:, cut], VG[:, cut], ALU.add).then_inc(sem("y_summed"), 1)

        @block.tensor
        def _(pe):
            mm = nc.tensor.matmul
            turn = [0]

            def bank(name):
                n = TILE_AT[name]
                assert n == turn[0], (name, TILES[turn[0]])
                turn[0] += 1
                if n >= BANKS:
                    before, eng = TILES[n - BANKS]
                    pe.wait_ge(sem(f"emptied_{eng}"), TURN[before])
                return ps[n % BANKS]

            def done(ins):
                ins.then_inc(sem("tile_done"), 1)

            def row_sums(name):
                i, row, _, _, _ = SECTION[name]
                for j in range(2):
                    w = piece(f"ada{i + j}").rearrange("p (k n) -> p k n", k=KC)
                    o = bank(f"{name}{j}")
                    piece_landed(pe, f"ada{i + j}")
                    for k in range(KC):
                        q = k % 4 * 32
                        ins = mm(o[q:q + 32, :], condr[:, k, :], w[:, k, :], start=(k < 4), stop=(k >= KC - 4))
                    done(ins)

            def spread(name):
                row = SECTION[name][1]
                pe.wait_ge(sem(f"{name}_row"), 2)
                for c in range(2):
                    for j in range(2):
                        o = bank(f"{name}_row{c}{j}")
                        done(mm(o[:, :], cols[:, 9 + c:10 + c].broadcast_to([P, P]), row[:, j * 512:(j + 1) * 512], start=True, stop=True))

            def section(name):
                row_sums(name)
                spread(name)

            pe.wait_ge(sem("consts_in"), 16)
            pe.wait_ge(sem("cond_ready"), 2)
            section("sc1")
            section("sh1")

            def transposed(n):
                for t in range(TT):
                    pe.wait_ge(sem(f"h{n}_ready"), t + 1)
                    for half in range(2):
                        o = bank(f"h{n}T{t}{half}")
                        for k in range(4):
                            kk = half * 4 + k
                            ins = nc.tensor.transpose(o[:, k * P:(k + 1) * P], HN[n][t][:, kk * P:(kk + 1) * P], ident)
                        done(ins)

            transposed(1)
            emptied(pe, "h1T20")
            emptied(pe, "h1T21")

            def features(tile, w, m, rhs, kc):
                o = bank(tile)
                for k in range(kc):
                    ins = mm(o[:, 0:T], w[:, k, m * P:(m + 1) * P], rhs[:, k, :], start=(k == 0), stop=(k == kc - 1))
                done(ins)

            for g in range(G):
                if g % 4 == 0:
                    piece_landed(pe, f"win{g // 4}")
                features(f"uf{g}", piece(f"win{g // 4}").rearrange("p (k n) -> p k n", k=KC), g % 4, hT, KC)

            for g in range(G + 1):
                if g < G:
                    emptied(pe, f"uf{g}")
                    for tiles, part in (((0, 1), "a"), ((2,), "b")):
                        o = bank(f"chan{g}{part}")
                        for n, t in enumerate(tiles):
                            ins = mm(o[:, n * 256:(n + 1) * 256], uT[:, g, t * P:(t + 1) * P], const("dft_chan"), start=True, stop=True)
                        done(ins)
                if g > 0:
                    gg = g - 1
                    emptied(pe, f"chan{gg}b")
                    a = AB[:, gg % 2, :].rearrange("p (t n) -> p t n", t=TT)
                    o = bank(f"pos{gg}")
                    cctx = const("dft_ctx")
                    clat = const("dft_lat")
                    for s in range(2):
                        mm(o[:, 0:CTX], a[:, 0, s * P:(s + 1) * P], cctx[:, s * P:(s + 1) * P], start=(s == 0), stop=(s == 1))
                    for n in range(4):
                        tc, s = n // 2, n % 2
                        ins = mm(o[:, CTX:T], a[:, 1 + tc, s * P:(s + 1) * P], clat[:, n * LAT:(n + 1) * LAT], start=(n == 0), stop=(n == 3))
                    done(ins)

            for i, name in enumerate(("q", "k", "v", "sw")):
                w = piece(f"win{2 + i}").rearrange("p (k n) -> p k n", k=KC)
                piece_landed(pe, f"win{2 + i}")
                for t in range(TT):
                    o = bank(f"{name}{t}")
                    for k in range(KC):
                        ins = mm(o[:, :], hT[:, k, t * P:(t + 1) * P], w[:, k, :], start=(k == 0), stop=(k == KC - 1))
                    done(ins)

            for t in range(TT):
                for name, nat in (("q", q_nat), ("k", k_nat)):
                    if t:
                        pe.wait_ge(sem(f"{name}_rotated"), t)
                    else:
                        emptied(pe, f"{name}0")
                    o = bank(f"{name}T{t}")
                    for h in range(H):
                        ins = nc.tensor.transpose(o[:, h * P:(h + 1) * P], nat[:, t, h * P:(h + 1) * P], ident)
                    done(ins)
            emptied(pe, "v2")
            for d in range(2):
                pe.wait_ge(sem("kw_ready"), d + 1)
                o = bank(f"state{d}")
                for h in range(H):
                    ins = mm(o[:, h * P:(h + 1) * P], kw[:, d, h * P:(h + 1) * P], v_nat[:, 0, h * P:(h + 1) * P], start=True, stop=True)
                done(ins)
            emptied(pe, "qT2")
            emptied(pe, "kT2")
            o = bank("sc_ctx")
            for h in range(H):
                ins = mm(o[:, h * P:(h + 1) * P], kT[:, h, 0:P], qT[:, h, 0:P], start=True, stop=True)
            done(ins)
            for h in range(H):
                o = bank(f"sc_lat{h}")
                for j in range(2):
                    ins = mm(o[:, j * LAT:(j + 1) * LAT], kT[:, h, (1 + j) * P:(2 + j) * P], qT[:, h, CTX:T], start=True, stop=True)
                done(ins)
            emptied(pe, "sc_ctx")
            o = bank("o0")
            for h in range(H):
                ins = mm(o[:, h * P:(h + 1) * P], sc_sb[:, 4, h * P:(h + 1) * P], v_nat[:, 0, h * P:(h + 1) * P], start=True, stop=True)
            done(ins)
            pe.wait_ge(sem("state_in"), 32)
            for t in (1, 2):
                o = bank(f"o{t}")
                for h in range(H):
                    emptied(pe, f"sc_lat{h}")
                    for j in range(2):
                        ins = mm(o[:, h * P:(h + 1) * P], sc_sb[:, h, j * LAT + (t - 1) * P:j * LAT + t * P],
                                 v_nat[:, 1 + j, h * P:(h + 1) * P], start=(j == 0), stop=(j == 1))
                done(ins)
                for d, name in ((0, "cross_f"), (1, "cross_b")):
                    o = bank(f"{name}{t}")
                    for h in range(H):
                        ins = mm(o[:, h * P:(h + 1) * P], qT[:, h, t * P:(t + 1) * P], S0[:, d, h, :], start=True, stop=True)
                    done(ins)
            emptied(pe, "pos7")
            for m in range(KC):
                i = m // 4
                if m % 4 == 0:
                    piece_landed(pe, f"win{6 + i}")
                    piece_landed(pe, f"four{i}")
                features(f"gf{m}", piece(f"win{6 + i}").rearrange("p (k n) -> p k n", k=KC), m % 4, hT, KC)
                features(f"fo{m}", piece(f"four{i}").rearrange("p (k n) -> p k n", k=KC), m % 4, fmixT, G)
            for t in range(TT):
                pe.wait_ge(sem("ret_ready"), t + 1)
                o = bank(f"retT{t}")
                for h in range(H):
                    ins = nc.tensor.transpose(o[:, h * P:(h + 1) * P], g_nat[:, t, h * P:(h + 1) * P], ident)
                done(ins)
            emptied(pe, "retT2")
            for m in range(KC):
                i = m // 4
                if m % 4 == 0:
                    piece_landed(pe, f"win{8 + i}")
                if m == 0:
                    piece_landed(pe, "ret")
                features(f"gr{m}", piece(f"win{8 + i}").rearrange("p (k n) -> p k n", k=KC), m % 4, hT, KC)
                features(f"ro{m}", piece("ret").rearrange("p (k n) -> p k n", k=H), m, retT, H)

            section("g1")
            pe.wait_ge(sem("merged"), KC)
            for n in range(2):
                w = piece(f"out{n}").rearrange("p (k n) -> p k n", k=KC)
                piece_landed(pe, f"out{n}")
                for t in range(TT):
                    o = bank(f"mix{n}{t}")
                    for k in range(KC):
                        ins = mm(o[:, :], mergedT[:, k, t * P:(t + 1) * P], w[:, k, :], start=(k == 0), stop=(k == KC - 1))
                    done(ins)
            section("sc2")
            section("sh2")
            transposed(2)
            row_sums("g2")
            emptied(pe, "h2T20")
            emptied(pe, "h2T21")
            pe.wait_ge(sem("router_in"), 32)
            o = bank("logitsT")
            for k in range(KC):
                q = k % 2 * E
                ins = mm(o[q:q + E, 0:T], wr[:, k, :], hT[:, k, :], start=(k < 2), stop=(k >= KC - 2))
            done(ins)
            emptied(pe, "logitsT")
            o = bank("logits")
            for t in range(TT):
                ins = mm(o[:, t * E:(t + 1) * E], logitsT[:, t * P:(t + 1) * P], const("ident_pair"), start=True, stop=True)
            done(ins)
            spread("g2")

            def shared_hidden(t):
                w = piece("sgu").rearrange("p (k n) -> p k n", k=KC)
                o = bank(f"sgu{t}")
                for k in range(KC):
                    ins = mm(o[:, :], hT[:, k, t * P:(t + 1) * P], w[:, k, :], start=(k == 0), stop=(k == KC - 1))
                done(ins)

            def shared_down(t):
                emptied(pe, f"shT{t}")
                w = piece("sd")[:, 0:CELL].rearrange("p (j n) -> p j n", j=2)
                for n in range(2):
                    o = bank(f"sd{t}{n}")
                    for j in range(2):
                        ins = mm(o[:, :], shT_sb[:, t, j, :], w[:, j, n * 512:(n + 1) * 512], start=(j == 0), stop=(j == 1))
                    done(ins)

            def index_products(o, q, table, at):
                pe.wait_ge(sem("onehot_ready"), q + 1)
                for e in range(QUAD):
                    c = at + e
                    for t in range(TT):
                        for half in range(2):
                            ins = mm(o[half * SLOTS:(half + 1) * SLOTS, c * 6:c * 6 + 6], onehot[:, q % 2, t, e, :],
                                     table[:, t, c, :], start=(t == 0), stop=(t == TT - 1))
                return ins

            piece_landed(pe, "sgu")
            shared_hidden(0)
            pe.wait_ge(sem("cbf_ready"), 2)
            pe.wait_ge(sem("sel_ready"), 1)
            o = bank("rank")
            for t in range(TT):
                for u in range(t + 1):
                    ins = mm(o[:, t * E:(t + 1) * E], cbf[:, 0 if u == t else 1, :], sel_bf[:, u, :], start=(u == 0), stop=(u == t))
            done(ins)
            o = bank("count")
            for t in range(TT):
                ins = mm(o[0:E, 0:1], sel_bf[:, t, :], cbf[:, 1, 0:1], start=(t == 0), stop=(t == TT - 1))
            done(ins)
            shared_hidden(1)
            pe.wait_ge(sem("further_ready"), 1)
            done(mm(bank("start")[0:E, 0:1], cbf[0:E, 0, 0:E], further_bf[0:E, :], start=True, stop=True))
            pe.wait_ge(sem("start_ready"), 1)
            o = bank("table")
            mm(o[0:1, 0:E], further_n, ident[0:E, 0:E], start=True, stop=True)
            done(mm(o[0:1, E:2 * E], before_n, ident[0:E, 0:E], start=True, stop=True))
            for name, src, ready in (("rankT", r_rank, "rank_ready"), ("wT", r_w, "w_ready")):
                pe.wait_ge(sem(ready), 1)
                o = bank(name)
                for t in range(TT):
                    ins = nc.tensor.transpose(o[0:E, t * P:(t + 1) * P], src[:, t, :], ident)
                done(ins)
            emptied(pe, "wT")
            pe.wait_ge(sem("mine_ready"), 3)
            o = bank("rank_x")
            for t in range(TT):
                mm(o[:, t * FURTHER:(t + 1) * FURTHER], rankT[:, t * P:(t + 1) * P], mine, start=True, stop=False)
                ins = mm(o[:, t * FURTHER:(t + 1) * FURTHER], minus_slots, rounds, start=False, stop=True)
            done(ins)
            o = bank("w_x")
            for t in range(TT):
                ins = mm(o[:, t * FURTHER:(t + 1) * FURTHER], wT[:, t * P:(t + 1) * P], mine, start=True, stop=True)
            done(ins)
            shared_hidden(2)
            index = ps[TILE_AT["index"] % BANKS]
            emptied(pe, TILES[TILE_AT["index"] - BANKS][0])
            pe.wait_ge(sem("m6_ready"), 1)
            index_products(index, 0, M6, 0).then_inc(sem("onehot_used"), 1)
            for t in range(TT):
                emptied(pe, f"sgu{t}")
                o = bank(f"shT{t}")
                for j in range(2):
                    ins = nc.tensor.transpose(o[:, j * P:(j + 1) * P], s_hid[t][:, j:ED:2], ident)
                done(ins)
            index_products(index, 1, M6, QUAD).then_inc(sem("onehot_used"), 1)
            piece_landed(pe, "sd")
            shared_down(0)
            index_products(index, 2, M6, 2 * QUAD).then_inc(sem("onehot_used"), 1)
            bank("index")
            done(index_products(index, 3, M6, 3 * QUAD))
            o = bank("further")
            pe.wait_ge(sem("m6x_ready"), 1)
            done(index_products(o, E // QUAD, M6X, 0))
            shared_down(1)
            shared_down(2)
            emptied(pe, "further")
            more = many(pe)
            with pe.If(more > 0):
                for q in range(1, FURTHER // QUAD):
                    index_products(o, E // QUAD + q, M6X, q * QUAD).then_inc(sem("more_index"), 1)
                pe.wait_ge(sem("more_index_out"), 1)
            emptied(pe, "sd21")
            pe.nop()


            def tokens(b, s, turn):
                par = s % 2
                pe.wait_ge(sem(f"gathered{s}"), turn)
                if not (isinstance(b, int) and b < 2):
                    pe.wait_ge(sem("xT_ready"), b - 1)
                for k in range(4):
                    ins = nc.tensor.transpose(ps[4 + par][:, k * P:(k + 1) * P], xg[s][:, k * P:(k + 1) * P], ident)
                ins.then_inc(sem("tokens_used"), 1)

            def gate_up(b, s, uses):
                par = s % 2
                wg, wu, _ = expert(s)
                pe.wait_ge(sem("xT_ready"), b + 1)
                pe.wait_ge(sem(f"gate_up_slot{s}"), uses)
                if not (isinstance(b, int) and b < 2):
                    pe.wait_ge(sem("hid_ready"), b - 1)
                for k in range(KC):
                    lhs = xT[par][:, k % 4, (k // 4) * SLOTS:(k // 4 + 1) * SLOTS]
                    mm(ps[par][0:SLOTS, 0:ED], lhs, wg[:, k, :], start=(k == 0), stop=(k == KC - 1))
                    ins = mm(ps[par][SLOTS:P, 0:ED], lhs, wu[:, k, :], start=(k == 0), stop=(k == KC - 1))
                ins.then_inc(sem("gate_up_done"), 1)

            def hidden_T(b, par):
                pe.wait_ge(sem("hid_ready"), b + 1)
                if not (isinstance(b, int) and b < 2):
                    pe.wait_ge(sem("hidT_ready"), b - 1)
                stand_alone(pe, "pe_passed")
                for j in range(2):
                    ins = nc.tensor.transpose(ps[6 + par][:, j * SLOTS:(j + 1) * SLOTS], hid[par][SLOTS:P, j:ED:2], ident[SLOTS:P, SLOTS:P])
                ins.then_inc(sem("hidT_done"), 1)

            def down(b, s, uses):
                par = s % 2
                _, _, wd = expert(s)
                pe.wait_ge(sem("hidT_ready"), b + 1)
                pe.wait_ge(sem(f"down_slot{s}"), uses)
                if not (isinstance(b, int) and b < 2):
                    pe.wait_ge(sem("y_ready"), b - 1)
                for j in range(2):
                    mm(ps[2 + par][0:SLOTS, :], hidT[par][:, j, :], wd[:, j, 0:512], start=(j == 0), stop=(j == 1))
                    ins = mm(ps[2 + par][SLOTS:P, :], hidT[par][:, j, :], wd[:, j, 512:1024], start=(j == 0), stop=(j == 1))
                ins.then_inc(sem("down_done"), 1)

            def further(e, i, s):
                par = s % 2
                wg, wu, wd = expert(s)

                def block(u):
                    pe.wait_ge(sem("f_gathered"), u * 16 + 16)
                    pe.wait_ge(sem("xT_ready"), e + 1)
                    for k in range(4):
                        ins = nc.tensor.transpose(ps[4 + par][:, k * P:(k + 1) * P], xg_f[:, k * P:(k + 1) * P], ident)
                    ins.then_inc(sem("f_tokens_used"), 1)
                    pe.wait_ge(sem("f_xT_ready"), u + 1)
                    pe.wait_ge(sem(f"gate_up_slot{s}"), i * 32 + 32)
                    pe.wait_ge(sem(f"down_slot{s}"), i * 16 + 16)
                    if not (isinstance(e, int) and e < 2):
                        pe.wait_ge(sem("y_ready"), e - 1)
                    stand_alone(pe, "pe_passed")
                    for k in range(KC):
                        lhs = xT_f[:, k % 4, (k // 4) * SLOTS:(k // 4 + 1) * SLOTS]
                        mm(ps[par][0:SLOTS, 0:ED], lhs, wg[:, k, :], start=(k == 0), stop=(k == KC - 1))
                        ins = mm(ps[par][SLOTS:P, 0:ED], lhs, wu[:, k, :], start=(k == 0), stop=(k == KC - 1))
                    ins.then_inc(sem("f_gate_up_done"), 1)
                    pe.wait_ge(sem("f_hid_ready"), u + 1)
                    stand_alone(pe, "pe_passed")
                    for j in range(2):
                        ins = nc.tensor.transpose(ps[6 + par][:, j * SLOTS:(j + 1) * SLOTS], hid_f[SLOTS:P, j:ED:2], ident[SLOTS:P, SLOTS:P])
                    ins.then_inc(sem("f_hidT_done"), 1)
                    pe.wait_ge(sem("f_hidT_ready"), u + 1)
                    for j in range(2):
                        mm(ps[2 + par][0:SLOTS, :], hidT_f[:, j, :], wd[:, j, 0:512], start=(j == 0), stop=(j == 1))
                        ins = mm(ps[2 + par][SLOTS:P, :], hidT_f[:, j, :], wd[:, j, 512:1024], start=(j == 0), stop=(j == 1))
                    ins.then_inc(sem("f_down_done"), 1)
                further_blocks(pe, e, block)

            def step(b, i, s, more):
                further(b, i, s)
                gate_up(b, s, i * 32 + 32)
                if more:
                    tokens(b + 1, (s + 1) % NSLOT, i * 16 + (32 if s == NSLOT - 1 else 16))
                if not (isinstance(b, int) and b == 0):
                    down(b - 1, (s - 1) % NSLOT, i * 16 + (16 if s else 0))
                hidden_T(b, s % 2)

            tokens(0, 0, 16)
            for b in range(NSLOT):
                step(b, 0, b, True)
            with pe.Fori(1, E // NSLOT - 1) as i:
                for s in range(NSLOT):
                    step(i * NSLOT + s, i, s, True)
            for b in range(E - NSLOT, E):
                step(b, E // NSLOT - 1, b % NSLOT, b + 1 < E)
            down(E - 1, NSLOT - 1, 16 * (E // NSLOT))
        @block.scalar
        def _(act):
            chain = [0]
            turns = [0]

            def link(ins):
                chain[0] += 1
                ins.then_inc(sem("act_chain"), 1)
                act.wait_ge(sem("act_chain"), chain[0])

            def tile(name):
                act.wait_ge(sem("tile_done"), TILE_AT[name] + 1)
                return ps[TILE_AT[name] % BANKS]

            def emptied_by(ins, name):
                assert TURN[name] == turns[0] + 1, name
                turns[0] += 1
                ins.then_inc(sem("emptied_A"), 1)

            def spread(name):
                rows = SECTION[name][4]
                for c in range(2):
                    for j in range(2):
                        n = f"{name}_row{c}{j}"
                        o = tile(n)
                        emptied_by(nc.scalar.copy(rows[:, c, j * 512:(j + 1) * 512], o[:, :]), n)

            act.wait_ge(sem("cond_in"), 32)
            for c in range(2):
                nc.scalar.activation(condr[:, :, c::2], cond[:, c, :].unsqueeze(2).broadcast_to([P, KC, 16]), ACT.Silu).then_inc(sem("cond_ready"), 1)
            act.wait_ge(sem("x_in"), 32)
            for t in range(TT):
                if t:
                    act.wait_ge(sem("ssq1"), t)
                nc.scalar.activation(junk[1], x[:, t, :], ACT.Square, accum_out=ssq[:, t:t + 1]).then_inc(sem("ssq1"), 1)
            act.wait_ge(sem("var1"), 1)
            nc.scalar.activation(rstd, rstd, ACT.Sqrt).then_inc(sem("std1"), 1)
            spread("sh1")

            def hT_half(n):
                for t in range(TT):
                    name = f"h{n}T{t}0"
                    o = tile(name)
                    emptied_by(nc.scalar.copy(hT[:, 0:4, t * P:(t + 1) * P], o[:, :].rearrange("p (k t) -> p k t", k=4)), name)

            hT_half(1)
            for g in range(G):
                name = f"uf{g}"
                o = tile(name)
                emptied_by(nc.scalar.copy(uT[:, g, :], o[:, 0:T]), name)
            for g in range(G):
                name = f"pos{g}"
                o = tile(name)
                emptied_by(nc.scalar.copy(fmixT[:, g, :], o[:, 0:T]), name)
            act.wait_ge(sem("dec_abs"), 1)
            nc.scalar.activation(s8[:, 1, :], s8[:, 0, :], ACT.Exp, scale=-1.0).then_inc(sem("dec_exp"), 1)
            act.wait_ge(sem("dec_u"), 1)
            nc.scalar.activation(s8[:, 3, :], s8[:, 2, :], ACT.Ln).then_inc(sem("dec_ln"), 1)
            act.wait_ge(sem("dec_args"), 1)
            nc.scalar.activation(DTf, DTf, ACT.Exp).then_inc(sem("decays"), 1)
            nc.scalar.activation(pw, pw, ACT.Exp).then_inc(sem("decays"), 1)
            for t in range(TT):
                o = tile(f"v{t}")
                emptied_by(nc.scalar.copy(v_nat[:, t, :], o[:, :]), f"v{t}")
            for t in range(TT):
                o = tile(f"sw{t}")
                emptied_by(nc.scalar.activation(g_nat[:, t, :], o[:, :], ACT.Silu), f"sw{t}")
            act.wait_ge(sem("pads_written"), 48)
            act.wait_ge(sem("f_scattered"), 16)
            for t in range(TT):
                o = tile(f"qT{t}")
                emptied_by(nc.scalar.mul(qT[:, :, t * P:(t + 1) * P], o[:, :].rearrange("p (h t) -> p h t", h=H), float(P) ** -0.5), f"qT{t}")
            for d in range(2):
                o = tile(f"state{d}")
                emptied_by(nc.scalar.copy(state_sb[:, d, :, :], o[:, :].rearrange("p (h e) -> p h e", h=H)), f"state{d}")
            for t in range(TT):
                act.wait_ge(sem("head_var"), t + 1)
                nc.scalar.activation(hst[:, 3 * t + 1, :], hst[:, 3 * t + 1, :], ACT.Sqrt).then_inc(sem("head_std"), 1)
            for kind in ("gf", "gr"):
                for m in range(KC):
                    n = m + (KC if kind == "gr" else 0)
                    if n >= 2:
                        emptied(act, f"{'fo' if n - 2 < KC else 'ro'}{(n - 2) % KC}")
                    o = tile(f"{kind}{m}")
                    emptied_by(nc.scalar.activation(tmpg[:, m % 2, :], o[:, 0:T], ACT.Sigmoid), f"{kind}{m}")
            spread("g1")
            for t in range(TT):
                act.wait_ge(sem("x1_ready"), t + 1)
                if t:
                    act.wait_ge(sem("ssq2"), t)
                nc.scalar.activation(junk[2], x[:, t, :], ACT.Square, accum_out=ssq[:, t:t + 1]).then_inc(sem("ssq2"), 1)
            spread("sh2")
            act.wait_ge(sem("var2"), 1)
            nc.scalar.activation(rstd, rstd, ACT.Sqrt).then_inc(sem("std2"), 1)
            hT_half(2)
            o = tile("logitsT")
            emptied_by(nc.scalar.copy(logitsT, o[:, 0:T]), "logitsT")
            o = tile("logits")
            emptied_by(nc.scalar.activation(r_score, o[:, 0:TT * E].rearrange("p (t e) -> p t e", t=TT), ACT.Sigmoid), "logits")
            spread("g2")

            def shared_silu(t):
                o = tile(f"sgu{t}")
                if t:
                    emptied(act, f"sgu{t - 1}")
                nc.scalar.activation(s_silu, o[:, 0:ED], ACT.Silu).then_inc(sem("ssilu_ready"), 1)

            shared_silu(0)
            shared_silu(1)
            for name, dst in (("rankT", rankT), ("wT", wT)):
                o = tile(name)
                emptied_by(nc.scalar.copy(dst, o[0:E, 0:T]), name)
            shared_silu(2)
            for t in range(TT):
                o = tile(f"shT{t}")
                emptied_by(nc.scalar.copy(shT_sb[:, t, :, :], o[:, 0:ED].rearrange("p (j t) -> p j t", j=2)), f"shT{t}")
            act.wait_ge(sem("h2_written"), 16 * TT)
            o = tile("index")
            emptied_by(nc.scalar.copy(index_sb, o[:, 0:E * 6].rearrange("p (e n) -> p e n", n=6)), "index")
            o = tile("further")
            emptied_by(nc.scalar.copy(further_sb[:, 0:QUAD, :], o[:, 0:QUAD * 6].rearrange("p (e n) -> p e n", n=6)), "further")
            act.wait_ge(sem("index_ready"), 5)
            act.wait_ge(sem("further_index_ready"), 1)
            act.wait_ge(sem("table_ready"), 1)

            def silu(b, par):
                act.wait_ge(sem("gate_up_done"), b + 1)
                if not (isinstance(b, int) and b < 2):
                    act.wait_ge(sem("hid_ready"), b - 1)
                nc.scalar.activation(sg[par][SLOTS:P, :], ps[par][0:SLOTS, 0:ED], ACT.Silu).then_inc(sem("silu_ready"), 1)

            def outputs(b, s):
                act.wait_ge(sem("down_done"), b + 1)
                if not (isinstance(b, int) and b < NSLOT):
                    act.wait_ge(sem(f"scattered{s % 2}"), (b - s % 2) * 8 - 16)
                nc.scalar.activation(yb[s], ps[2 + s % 2][:, :], ACT.Copy, scale=column(cw, b)).then_inc(sem("y_ready"), 1)

            def further(e, par):
                def block(u):
                    act.wait_ge(sem("f_gate_up_done"), u + 1)
                    nc.scalar.activation(sg_f[SLOTS:P, :], ps[par][0:SLOTS, 0:ED], ACT.Silu).then_inc(sem("f_silu_ready"), 1)
                    act.wait_ge(sem("f_down_done"), u + 1)
                    act.wait_ge(sem("f_scattered"), u * 16 + 16)
                    nc.scalar.activation(yb_f, ps[2 + par][:, :], ACT.Copy, scale=column(cw, u + E)).then_inc(sem("f_y_ready"), 1)
                further_blocks(act, e, block)

            def step(b, s):
                further(b, s % 2)
                silu(b, s % 2)
                if not (isinstance(b, int) and b == 0):
                    outputs(b - 1, (s - 1) % NSLOT)

            for b in range(2 * NSLOT):
                step(b, b % NSLOT)
            with act.Fori(2, E // NSLOT) as i:
                for s in range(NSLOT):
                    step(i * NSLOT + s, s)
            outputs(E - 1, (E - 1) % NSLOT)
            for t in range(TT):
                act.wait_ge(sem("x2_ready"), t + 1)
                nc.scalar.activation(junk[3], x[:, t, :], ACT.Square, accum_out=ssq[:, t:t + 1]).then_inc(sem("ssq3"), 1)
                act.wait_ge(sem("var3"), t + 1)
                nc.scalar.activation(rstd[:, t:t + 1], rstd[:, t:t + 1], ACT.Sqrt).then_inc(sem("std3"), 1)

        @block.vector
        def _(dve):
            v = nc.vector
            chain = [0]
            turns = [0]

            def link(ins):
                chain[0] += 1
                ins.then_inc(sem("vec_chain"), 1)
                dve.wait_ge(sem("vec_chain"), chain[0])

            def tile(name):
                dve.wait_ge(sem("tile_done"), TILE_AT[name] + 1)
                return ps[TILE_AT[name] % BANKS]

            def emptied_by(ins, name):
                assert TURN[name] == turns[0] + 1, name
                turns[0] += 1
                ins.then_inc(sem("emptied_V"), 1)

            def section(name):
                _, row, bias, gain, rows = SECTION[name]
                for j in range(2):
                    cut = slice(j * 512, (j + 1) * 512)
                    o = tile(f"{name}{j}")
                    emptied_by(v.tensor_copy(row[:, cut], o[:, :]), f"{name}{j}")
                    dve.wait_ge(sem("emptied_V"), turns[0])
                    if j == 0:
                        dve.wait_ge(sem(f"{name}_bias_in"), 16 if gain is None else 32)
                    v.tensor_tensor(row[0:2, cut], row[0:2, cut], bias[:, cut], ALU.add).then_inc(sem(f"{name}_row"), 1)
                if gain is not None:
                    for c in range(2):
                        for j in range(2):
                            cut = slice(j * 512, (j + 1) * 512)
                            o = tile(f"{name}_row{c}{j}")
                            emptied_by(v.scalar_tensor_tensor(rows[:, c, cut], o[:, :], 1.0, gain[:, cut], ALU.add, ALU.mult), f"{name}_row{c}{j}")

            dve.wait_ge(sem("ssq1"), TT)
            v.tensor_scalar(rstd, ssq, 1.0 / D, EPS, ALU.mult, ALU.add).then_inc(sem("var1"), 1)
            dve.wait_ge(sem("std1"), 1)
            link(v.reciprocal(rstd, rstd))

            def modulate(n, scale, shift):
                dve.wait_ge(sem("emptied_V"), TURN[f"{scale}_row11"])
                rs, rh = SECTION[scale][4], SECTION[shift][4]
                for t in range(TT):
                    c = 0 if t == 0 else 1
                    link(v.scalar_tensor_tensor(work[:, :], x[:, t, :], rstd[:, t:t + 1], rs[:, c, :], ALU.mult, ALU.mult))
                    v.tensor_tensor(HN[n][t].rearrange("p (k q) -> p k q", k=KC), work[:, :].rearrange("p (q k) -> p k q", k=KC),
                                    rh[:, c, :].rearrange("p (q k) -> p k q", k=KC), ALU.add).then_inc(sem(f"h{n}_ready"), 1)
                    dve.wait_ge(sem(f"h{n}_ready"), t + 1)

            def hT_half(n):
                for t in range(TT):
                    name = f"h{n}T{t}1"
                    o = tile(name)
                    ins = v.tensor_copy(hT[:, 4:8, t * P:(t + 1) * P], o[:, :].rearrange("p (k t) -> p k t", k=4))
                    emptied_by(ins, name)

            section("sc1")
            section("sh1")
            dve.wait_ge(sem("emptied_A"), TURN["sh1_row11"])
            modulate(1, "sc1", "sh1")
            hT_half(1)
            for g in range(G):
                a = AB[:, g % 2, :]
                if g >= 2:
                    dve.wait_ge(sem("tile_done"), TILE_AT[f"pos{g - 2}"] + 1)
                o = tile(f"chan{g}a")
                emptied_by(v.tensor_copy(a[:, 0:512], o[:, :]), f"chan{g}a")
                o = tile(f"chan{g}b")
                emptied_by(v.tensor_copy(a[:, 512:768], o[:, 0:256]), f"chan{g}b")
            dve.wait_ge(sem("decay_in"), 32)
            link(v.tensor_scalar(s8[:, 1, :], dec, -1.0, None, ALU.mult))
            v.tensor_tensor(s8[:, 0, :], dec, s8[:, 1, :], ALU.max).then_inc(sem("dec_abs"), 1)
            dve.wait_ge(sem("dec_exp"), 1)
            v.tensor_scalar(s8[:, 2, :], s8[:, 1, :], 1.0, None, ALU.add).then_inc(sem("dec_u"), 1)
            dve.wait_ge(sem("dec_u"), 1)
            link(v.tensor_scalar(s8[:, 4, :], s8[:, 2, :], -1.0, None, ALU.add))
            link(v.tensor_scalar(s8[:, 5, :], s8[:, 4, :], 0.0, None, ALU.is_equal))
            link(v.tensor_tensor(s8[:, 4, :], s8[:, 4, :], s8[:, 5, :], ALU.add))
            link(v.reciprocal(s8[:, 6, :], s8[:, 4, :]))
            link(v.tensor_tensor(s8[:, 5, :], s8[:, 5, :], s8[:, 1, :], ALU.mult))
            dve.wait_ge(sem("dec_ln"), 1)
            link(v.tensor_tensor(s8[:, 7, :], s8[:, 3, :], s8[:, 1, :], ALU.mult))
            link(v.tensor_tensor(s8[:, 7, :], s8[:, 7, :], s8[:, 6, :], ALU.mult))
            link(v.tensor_tensor(s8[:, 7, :], s8[:, 7, :], s8[:, 5, :], ALU.add))
            link(v.tensor_scalar(s8[:, 8, :], dec, 0.0, None, ALU.min))
            link(v.tensor_tensor(lg, s8[:, 8, :], s8[:, 7, :], ALU.subtract))
            dve.wait_ge(sem("consts_in"), 16)
            dve.wait_ge(sem("dist_in"), 16)
            for h in range(H):
                link(v.tensor_scalar(DT[:, h, :], dist[:, 0:3 * P], lg[:, h:h + 1], None, ALU.mult))
                link(v.scalar_tensor_tensor(DT[:, h, :], dist[:, 3 * P:6 * P], lg[:, H + h:H + h + 1], DT[:, h, :], ALU.mult, ALU.add))
            for c in range(6):
                d = 0 if c in (0, 1, 4) else H
                ins = v.tensor_scalar(pw[:, c, :], lg[:, d:d + H], cols[:, c:c + 1], None, ALU.mult)
                if c < 5:
                    link(ins)
            ins.then_inc(sem("dec_args"), 1)
            v.tensor_copy(cbf[:, 0, :], const("before")).then_inc(sem("cbf_ready"), 1)
            v.memset(cbf[:, 1, :], 1.0).then_inc(sem("cbf_ready"), 1)

            for name, nat in (("q", q_nat), ("k", k_nat)):
                for t in range(TT):
                    o = tile(f"{name}{t}")
                    if t == 0:
                        emptied_by(v.tensor_copy(nat[:, 0, :], o[:, :]), f"{name}{t}")
                        continue
                    cos = const("rope_cos")[:, (t - 1) * P:t * P]
                    sin = const("rope_sin")[:, (t - 1) * P:t * P]
                    cosb = cos.unsqueeze(1).broadcast_to([P, H, P])
                    sin4 = sin.rearrange("p (a b f) -> p a b f", a=2, b=2)
                    src = o[:, :].rearrange("p (h a b f) -> p h a b f", h=H, a=2, b=2)
                    dst = work[:, 0:512].rearrange("p (h a b f) -> p h a b f", h=H, a=2, b=2)
                    for s in range(2):
                        link(v.tensor_tensor(dst[:, :, :, s, :], src[:, :, :, 1 - s, :],
                                             sin4[:, :, s, :].unsqueeze(1).broadcast_to([P, H, 2, 32]), ALU.mult))
                    ins = v.tensor_tensor(work[:, 512:1024].rearrange("p (h n) -> p h n", h=H), o[:, :].rearrange("p (h n) -> p h n", h=H), cosb, ALU.mult)
                    emptied_by(ins, f"{name}{t}")
                    dve.wait_ge(sem("emptied_V"), turns[0])
                    v.tensor_tensor(nat[:, t, :], work[:, 0:512], work[:, 512:1024], ALU.add).then_inc(sem(f"{name}_rotated"), 1)
                    dve.wait_ge(sem(f"{name}_rotated"), t)
            dve.wait_ge(sem("decays"), 2)
            for t in range(TT):
                o = tile(f"kT{t}")
                emptied_by(v.tensor_copy(kT[:, :, t * P:(t + 1) * P], o[:, :].rearrange("p (h t) -> p h t", h=H)), f"kT{t}")
            for d in range(2):
                v.tensor_tensor(kw[:, d, :].rearrange("p (h n) -> p h n", h=H), k_nat[:, 0, :].rearrange("p (h n) -> p h n", h=H),
                                pw[:, 4 + d, :].unsqueeze(2).broadcast_to([P, H, P]), ALU.mult).then_inc(sem("kw_ready"), 1)
            dve.wait_ge(sem("kw_ready"), 2)
            o = tile("sc_ctx")
            emptied_by(v.tensor_tensor(sc_sb[:, 4, :].rearrange("p (h n) -> p h n", h=H), o[:, :].rearrange("p (h n) -> p h n", h=H),
                                       DT[:, :, P:2 * P], ALU.mult), "sc_ctx")
            for h in range(H):
                o = tile(f"sc_lat{h}")
                link(v.tensor_tensor(sc_sb[:, h, 0:LAT], o[:, 0:LAT], DT[:, h, P:3 * P], ALU.mult))
                emptied_by(v.tensor_tensor(sc_sb[:, h, LAT:2 * LAT], o[:, LAT:2 * LAT], DT[:, h, 0:2 * P], ALU.mult), f"sc_lat{h}")
            hn = lambda a: a.rearrange("p (h n) -> p h n", h=H)
            spread4 = lambda a: a.unsqueeze(2).broadcast_to([P, H, P])
            for t in range(TT):
                ow, sq = work[:, 0:512], work[:, 512:1024]
                o = tile(f"o{t}")
                emptied_by(v.tensor_copy(ow, o[:, :]), f"o{t}")
                dve.wait_ge(sem("emptied_V"), turns[0])
                if t:
                    for d, name in ((0, "cross_f"), (1, "cross_b")):
                        o = tile(f"{name}{t}")
                        ins = v.tensor_tensor(hn(sq), hn(o[:, :]), spread4(pw[:, 2 * d + t - 1, :]), ALU.mult)
                        emptied_by(ins, f"{name}{t}")
                        dve.wait_ge(sem("emptied_V"), turns[0])
                        link(v.tensor_tensor(ow, ow, sq, ALU.add))
                mean, var, rs = hst[:, 3 * t, :], hst[:, 3 * t + 1, :], hst[:, 3 * t + 2, :]
                link(v.tensor_reduce(mean, hn(ow), AX.X, ALU.add))
                link(v.tensor_scalar(mean, mean, 1.0 / P, None, ALU.mult))
                link(v.tensor_tensor(hn(ow), hn(ow), spread4(mean), ALU.subtract))
                link(v.tensor_tensor(sq, ow, ow, ALU.mult))
                link(v.tensor_reduce(var, hn(sq), AX.X, ALU.add))
                v.tensor_scalar(var, var, 1.0 / P, EPS, ALU.mult, ALU.add).then_inc(sem("head_var"), 1)
                dve.wait_ge(sem("head_std"), t + 1)
                link(v.reciprocal(rs, var))
                link(v.tensor_tensor(hn(ow), hn(ow), spread4(rs), ALU.mult))
                if t == 0:
                    emptied(dve, "sw2")
                v.tensor_tensor(g_nat[:, t, :], g_nat[:, t, :], ow, ALU.mult).then_inc(sem("ret_ready"), 1)
                dve.wait_ge(sem("ret_ready"), t + 1)
            for m in range(KC):
                o = tile(f"fo{m}")
                dve.wait_ge(sem("emptied_A"), TURN[f"gf{m}"])
                ins = v.tensor_tensor(mergedT[:, m, :], o[:, 0:T], tmpg[:, m % 2, :], ALU.mult)
                emptied_by(ins, f"fo{m}")
            dve.wait_ge(sem("gn_in"), 16)
            for t in range(TT):
                o = tile(f"retT{t}")
                emptied_by(v.tensor_tensor(retT[:, :, t * P:(t + 1) * P], hn(o[:, :]), spread4(gn_col), ALU.mult), f"retT{t}")
            for m in range(KC):
                o = tile(f"ro{m}")
                dve.wait_ge(sem("emptied_A"), TURN[f"gr{m}"])
                ins = v.tensor_tensor(work[:, 0:T], o[:, 0:T], tmpg[:, m % 2, :], ALU.mult)
                emptied_by(ins, f"ro{m}")
                dve.wait_ge(sem("emptied_V"), turns[0])
                v.tensor_tensor(mergedT[:, m, :], mergedT[:, m, :], work[:, 0:T], ALU.add).then_inc(sem("merged"), 1)
                dve.wait_ge(sem("merged"), m + 1)
            section("g1")
            dve.wait_ge(sem("emptied_A"), TURN["g1_row11"])
            for n in range(2):
                for t in range(TT):
                    cut = slice(n * 512, (n + 1) * 512)
                    o = tile(f"mix{n}{t}")
                    ins = v.tensor_tensor(work[:, 0:512], o[:, :], SECTION["g1"][4][:, 0 if t == 0 else 1, cut], ALU.mult)
                    emptied_by(ins, f"mix{n}{t}")
                    dve.wait_ge(sem("emptied_V"), turns[0])
                    ins = v.tensor_tensor(x[:, t, cut], x[:, t, cut], work[:, 0:512], ALU.add)
                    if n:
                        ins.then_inc(sem("x1_ready"), 1)
                        dve.wait_ge(sem("x1_ready"), t + 1)
                    else:
                        link(ins)
            section("sc2")
            section("sh2")
            dve.wait_ge(sem("ssq2"), TT)
            v.tensor_scalar(rstd, ssq, 1.0 / D, EPS, ALU.mult, ALU.add).then_inc(sem("var2"), 1)
            dve.wait_ge(sem("std2"), 1)
            link(v.reciprocal(rstd, rstd))
            dve.wait_ge(sem("emptied_A"), TURN["sh2_row11"])
            modulate(2, "sc2", "sh2")
            hT_half(2)
            section("g2")

            dve.wait_ge(sem("emptied_A"), TURN["logits"])
            dve.wait_ge(sem("router_in"), 32)
            link(v.tensor_tensor(r_bias, r_score, bias_row[:, :].unsqueeze(1).broadcast_to([P, TT, E]), ALU.add))
            m8 = rg[:, 0:192].rearrange("p (t g n) -> p t g n", t=TT, g=EG)
            for t in range(TT):
                for g in range(EG):
                    ins = v.max(m8[:, t, g, :], r_bias[:, t, g * 8:(g + 1) * 8])
            link(ins)
            gs = rg[:, 192:216].rearrange("p (t g) -> p t g", t=TT)
            link(v.tensor_tensor(gs, m8[:, :, :, 0], m8[:, :, :, 1], ALU.add))
            own = gs.unsqueeze(3).broadcast_to([P, TT, EG, EG])
            other = gs.unsqueeze(2).broadcast_to([P, TT, EG, EG])
            gt = rg[:, 256:448].rearrange("p (t a b) -> p t a b", t=TT, a=EG)
            eq = rg[:, 512:704].rearrange("p (t a b) -> p t a b", t=TT, a=EG)
            v.tensor_tensor(gt, other, own, ALU.is_gt)
            link(v.tensor_tensor(eq, other, own, ALU.is_equal))
            link(v.tensor_tensor(eq, eq, const("tie").rearrange("p (a b) -> p a b", a=EG).unsqueeze(1).broadcast_to([P, TT, EG, EG]), ALU.mult))
            link(v.tensor_tensor(gt, gt, eq, ALU.add))
            gr = rg[:, 216:240].rearrange("p (t g) -> p t g", t=TT)
            link(v.tensor_reduce(gr, gt, AX.X, ALU.add))
            gm = rg[:, 448:472].rearrange("p (t g) -> p t g", t=TT)
            link(v.tensor_scalar(gm, gr, float(TOPG), None, ALU.is_lt))
            gp = rg[:, 472:496].rearrange("p (t g) -> p t g", t=TT)
            v.tensor_scalar(gp, gm, BIG, -BIG, ALU.mult, ALU.add)
            g4 = lambda a: a.rearrange("p t (g n) -> p t g n", g=EG)
            over8 = lambda a: a.unsqueeze(3).broadcast_to([P, TT, EG, 8])
            link(v.tensor_tensor(g4(r_mask), g4(r_bias), over8(gm), ALU.mult))
            link(v.tensor_tensor(g4(r_mask), g4(r_mask), over8(gp), ALU.add))
            top = rg[:, 704:728].rearrange("p (t n) -> p t n", t=TT)
            for t in range(TT):
                ins = v.max(top[:, t, :], r_mask[:, t, :])
            link(ins)
            for t in range(TT):
                ins = v.match_replace(r_rep[:, t, :], top[:, t, :], r_mask[:, t, :], BIG)
            link(ins)
            link(v.tensor_scalar(r_sel, r_rep, BIG, None, ALU.is_equal))
            v.tensor_copy(sel_bf[:, :, :], r_sel).then_inc(sem("sel_ready"), 1)
            link(v.tensor_tensor(r_w, r_score, r_sel, ALU.mult))
            ws = rg[:, 728:731]
            link(v.tensor_reduce(ws, r_w, AX.X, ALU.add))
            link(v.reciprocal(rg[:, 732:735], ws))
            v.scalar_tensor_tensor(r_w, r_w, ROUTED_SCALE, rg[:, 732:735].unsqueeze(2).broadcast_to([P, TT, E]), ALU.mult, ALU.mult).then_inc(sem("w_ready"), 1)
            dve.wait_ge(sem("w_ready"), 1)
            def brings(table, weights, done):
                v.tensor_copy(table[:, :, :, 1], cols[:, 8:9].unsqueeze(1).broadcast_to([P, TT, E]))
                v.memset(table[:, :, :, 2], 1.0)
                for t in range(TT):
                    v.memset(table[:, t, :, 0], float(P * (t - TT)))
                link(v.tensor_copy(table[:, :, :, 3], weights))
                link(v.tensor_tensor(r_x, weights, table[:, :, :, 3], ALU.subtract))
                link(v.tensor_copy(table[:, :, :, 4], r_x))
                link(v.tensor_tensor(r_x, r_x, table[:, :, :, 4], ALU.subtract))
                v.tensor_copy(table[:, :, :, 5], r_x).then_inc(sem(done), 1)
                dve.wait_ge(sem(done), 1)

            dve.wait_ge(sem("emptied_A"), TURN["g2_row11"])
            brings(M6, r_w, "m6_ready")
            def shared_hidden(t):
                o = tile(f"sgu{t}")
                dve.wait_ge(sem("ssilu_ready"), t + 1)
                emptied_by(v.tensor_tensor(s_hid[t], s_silu, o[:, ED:2 * ED], ALU.mult), f"sgu{t}")

            shared_hidden(0)
            o = tile("rank")
            v.scalar_tensor_tensor(r_rank, o[:, 0:TT * E].rearrange("p (t e) -> p t e", t=TT), 1.0, r_sel, ALU.add, ALU.mult).then_inc(sem("rank_ready"), 1)
            dve.wait_ge(sem("rank_ready"), 1)
            emptied_by(v.memset(minus_slots, -float(SLOTS)), "rank")
            cnt = rg[0:E, 256:257]
            o = tile("count")
            emptied_by(v.tensor_copy(cnt, o[0:E, 0:1]), "count")
            dve.wait_ge(sem("emptied_V"), turns[0])
            link(v.tensor_scalar(rg[0:E, 264:269], const("over", E), cnt, None, ALU.is_lt))
            link(v.tensor_reduce(further_n, rg[0:E, 264:269], AX.X, ALU.add))
            v.tensor_copy(further_bf[0:E, :], further_n).then_inc(sem("further_ready"), 1)

            def onehots(q, ranks, at):
                if q >= 2:
                    dve.wait_ge(sem("onehot_used"), q - 1)
                for t in range(TT):
                    ins = v.tensor_tensor(onehot[:, q % 2, t, :, :],
                                          ranks[:, t, at:at + QUAD].unsqueeze(2).broadcast_to([P, QUAD, SLOTS]),
                                          const("slot").unsqueeze(1).broadcast_to([P, QUAD, SLOTS]), ALU.is_equal)
                ins.then_inc(sem("onehot_ready"), 1)

            onehots(0, r_rank, 0)
            shared_hidden(1)
            o = tile("start")
            emptied_by(v.tensor_copy(before_n, o[0:E, 0:1]), "start")
            dve.wait_ge(sem("emptied_V"), turns[0])
            v.scalar_tensor_tensor(end_n, before_n, 1.0, further_n, ALU.add, ALU.add).then_inc(sem("start_ready"), 1)
            slots = const("slot", E)
            v.tensor_scalar(since, slots, -1.0, before_n, ALU.add, ALU.is_ge).then_inc(sem("mine_ready"), 1)
            dve.wait_ge(sem("start_ready"), 1)
            dve.wait_ge(sem("mine_ready"), 1)
            v.scalar_tensor_tensor(mine, slots, end_n, since, ALU.is_lt, ALU.mult).then_inc(sem("mine_ready"), 1)
            dve.wait_ge(sem("mine_ready"), 2)
            v.scalar_tensor_tensor(rounds, slots, before_n, mine, ALU.subtract, ALU.mult).then_inc(sem("mine_ready"), 1)
            onehots(1, r_rank, QUAD)
            o = tile("table")
            link(v.tensor_copy(tab[0:1, 0:2 * E], o[0:1, 0:2 * E]))
            emptied_by(v.tensor_tensor(total, o[0:1, E - 1:E], tab[0:1, 2 * E - 1:2 * E], ALU.add), "table")
            dve.wait_ge(sem("emptied_V"), turns[0])
            link(v.tensor_copy(tab[0:1, 2 * E + 1:2 * E + 2], total))
            v.tensor_scalar(tab[0:1, 2 * E:2 * E + 1], total, float(QUAD), None, ALU.is_ge).then_inc(sem("table_ready"), 1)
            o = tile("rank_x")
            emptied_by(v.tensor_copy(rank_x, o[:, 0:TT * FURTHER].rearrange("p (t e) -> p t e", t=TT)), "rank_x")
            o = tile("w_x")
            emptied_by(v.tensor_copy(w_x, o[:, 0:TT * FURTHER].rearrange("p (t e) -> p t e", t=TT)), "w_x")
            shared_hidden(2)
            for q in range(2, E // QUAD):
                onehots(q, r_rank, q * QUAD)
            dve.wait_ge(sem("emptied_V"), turns[0])
            brings(M6X, w_x, "m6x_ready")
            onehots(E // QUAD, rank_x, 0)
            gate = [SECTION["g2"][4][:, 0 if t == 0 else 1, :] for t in range(TT)]

            def shared_out(t):
                for n in range(2):
                    cut = slice(n * 512, (n + 1) * 512)
                    o = tile(f"sd{t}{n}")
                    emptied_by(v.tensor_tensor(work[:, cut], o[:, :], gate[t][:, cut], ALU.mult), f"sd{t}{n}")
                dve.wait_ge(sem("emptied_V"), turns[0])
                link(v.tensor_tensor(x[:, t, :], x[:, t, :], work[:, :], ALU.add))

            shared_out(0)

            def rows_and_weights(src, at, n, done):
                a, b = work[:, 512:512 + n], work[:, 640:640 + n]
                v.tensor_tensor(a, src[:, :, 0], src[:, :, 1], ALU.add).then_inc(sem(done), 1)
                v.tensor_scalar(b, src[:, :, 2], cols[:, 7:8], cols[:, 6:7], ALU.mult, ALU.add).then_inc(sem(done), 1)
                dve.wait_ge(sem(done), 2)
                v.scalar_tensor_tensor(idx[:, at:at + n], a, 2.0, b, ALU.mult, ALU.add).then_inc(sem(done), 1)
                dve.wait_ge(sem(done), 3)
                v.tensor_tensor(a, src[:, :, 3], src[:, :, 4], ALU.add).then_inc(sem(done), 1)
                dve.wait_ge(sem(done), 4)
                v.tensor_tensor(cw[:, at:at + n], a, src[:, :, 5], ALU.add).then_inc(sem(done), 1)
                dve.wait_ge(sem(done), 5)

            dve.wait_ge(sem("emptied_A"), TURN["index"])
            rows_and_weights(index_sb, 0, E, "index_ready")
            dve.wait_ge(sem("emptied_A"), TURN["further"])
            rows_and_weights(further_sb[:, 0:QUAD, :], E, QUAD, "further_first_ready")
            more = many(dve)
            with dve.If(more > 0):
                for q in range(1, FURTHER // QUAD):
                    if q > 1:
                        dve.wait_ge(sem("more_index"), q - 1)
                    for t in range(TT):
                        ins = v.tensor_tensor(onehot[:, q % 2, t, :, :],
                                              rank_x[:, t, q * QUAD:(q + 1) * QUAD].unsqueeze(2).broadcast_to([P, QUAD, SLOTS]),
                                              const("slot").unsqueeze(1).broadcast_to([P, QUAD, SLOTS]), ALU.is_equal)
                    ins.then_inc(sem("onehot_ready"), 1)
                dve.wait_ge(sem("more_index"), FURTHER // QUAD - 1)
                v.tensor_copy(further_sb[:, QUAD:, :], ps[TILE_AT["further"] % BANKS][:, QUAD * 6:FURTHER * 6].rearrange("p (e n) -> p e n", n=6)).then_inc(sem("more_index_out"), 1)
                dve.wait_ge(sem("more_index_out"), 1)
                rows_and_weights(further_sb[:, QUAD:, :], E + QUAD, FURTHER - QUAD, "further_rest_ready")
            v.memset(work[:, 0:1], 0.0).then_inc(sem("further_index_ready"), 1)
            dve.wait_ge(sem("further_index_ready"), 1)
            shared_out(1)
            shared_out(2)

            def tokens(b, par):
                dve.wait_ge(sem("tokens_used"), b + 1)
                if not (isinstance(b, int) and b < 2):
                    dve.wait_ge(sem("gate_up_done"), b - 1)
                v.tensor_copy(xT[par], ps[4 + par][:, :].rearrange("p (k s) -> p k s", k=4)).then_inc(sem("xT_ready"), 1)

            def hidden(b, par):
                dve.wait_ge(sem("silu_ready"), b + 1)
                if not (isinstance(b, int) and b < 2):
                    dve.wait_ge(sem("hidT_done"), b - 1)
                v.tensor_tensor(hid[par][SLOTS:P, :], sg[par][SLOTS:P, :], ps[par][SLOTS:P, 0:ED], ALU.mult).then_inc(sem("hid_ready"), 1)

            def hidden_T(b, par):
                dve.wait_ge(sem("hidT_done"), b + 1)
                if not (isinstance(b, int) and b < 2):
                    dve.wait_ge(sem("down_done"), b - 1)
                v.tensor_copy(hidT[par], ps[6 + par][:, 0:2 * SLOTS].rearrange("p (j s) -> p j s", j=2)).then_inc(sem("hidT_ready"), 1)

            def further(e, par):
                def block(u):
                    dve.wait_ge(sem("f_tokens_used"), u + 1)
                    v.tensor_copy(xT_f, ps[4 + par][:, :].rearrange("p (k s) -> p k s", k=4)).then_inc(sem("f_xT_ready"), 1)
                    dve.wait_ge(sem("f_silu_ready"), u + 1)
                    v.tensor_tensor(hid_f[SLOTS:P, :], sg_f[SLOTS:P, :], ps[par][SLOTS:P, 0:ED], ALU.mult).then_inc(sem("f_hid_ready"), 1)
                    dve.wait_ge(sem("f_hidT_done"), u + 1)
                    v.tensor_copy(hidT_f, ps[6 + par][:, 0:2 * SLOTS].rearrange("p (j s) -> p j s", j=2)).then_inc(sem("f_hidT_ready"), 1)
                further_blocks(dve, e, block)

            def step(b, s, more):
                further(b, s % 2)
                if more:
                    tokens(b + 1, (s + 1) % 2)
                hidden(b, s % 2)
                hidden_T(b, s % 2)

            tokens(0, 0)
            for b in range(NSLOT):
                step(b, b, True)
            with dve.Fori(1, E // NSLOT - 1) as i:
                for s in range(NSLOT):
                    step(i * NSLOT + s, s, True)
            for b in range(E - NSLOT, E):
                step(b, b % NSLOT, b + 1 < E)
            dve.wait_ge(sem("y2_in"), 16)
            for t in range(TT):
                link(v.tensor_tensor(work[:, :], Fm[:, t * D:(t + 1) * D], gate[t], ALU.mult))
                link(v.tensor_tensor(x[:, t, :], x[:, t, :], work[:, :], ALU.add))

            def residual(t):
                cut = slice(t * D, (t + 1) * D)
                dve.wait_ge(sem(f"y_in{t}"), 32)
                if t == 0:
                    link(v.tensor_tensor(hTf[:, cut], hTf[:, cut], VG[:, cut], ALU.add))
                else:
                    dve.wait_ge(sem("y_summed"), t)
                link(v.tensor_tensor(work[:, :], hTf[:, cut], gate[t], ALU.mult))
                v.tensor_tensor(x[:, t, :], x[:, t, :], work[:, :], ALU.add).then_inc(sem("x2_ready"), 1)
                dve.wait_ge(sem("x2_ready"), t + 1)

            def final_norm(t):
                dve.wait_ge(sem("ssq3"), t + 1)
                v.tensor_scalar(rstd[:, t:t + 1], ssq[:, t:t + 1], 1.0 / D, EPS, ALU.mult, ALU.add).then_inc(sem("var3"), 1)
                dve.wait_ge(sem("std3"), t + 1)
                link(v.reciprocal(rstd[:, t:t + 1], rstd[:, t:t + 1]))
                v.scalar_tensor_tensor(x[:, t, :], x[:, t, :], rstd[:, t:t + 1], fin_g, ALU.mult, ALU.mult).then_inc(sem("out_ready"), 1)

            dve.wait_ge(sem("fin_in"), 16)
            residual(0)
            for t in range(1, TT):
                residual(t)
                final_norm(t - 1)
            final_norm(TT - 1)


_INS = ["x_prompt", "x_sample", "state_ret_fwd", "state_ret_bwd", "c", "c_ctx", "w_ada", "b_ada", "norm1_g", "norm2_g",
        "w_in", "ret_decay_fwd", "ret_decay_bwd", "ret_gn_g", "w_four_out", "w_ret_out", "w_out", "w_router",
        "router_bias", "w_exp_gate", "w_exp_up", "w_exp_down", "w_shared_gate", "w_shared_up", "w_shared_down",
        "final_norm_g"]
_OUTS = [(1, CTX, D), (1, LAT, D), (1, 1, H, P, P), (1, 1, H, P, P)]


def kernel(**inputs):
    from concourse import bacc
    from concourse.bass_utils import run_bass_kernel_spmd

    nc = bacc.Bacc("TRN2", target_bir_lowering=False, num_devices=1)
    arrays, args = {}, {}
    for name in _INS:
        a = np.ascontiguousarray(inputs[name])
        arrays[f"in_{name}"] = a
        args[name] = nc.dram_tensor(f"in_{name}", a.shape, mybir.dt.from_np(a.dtype), kind="ExternalInput").ap()
    table = constants()[0]
    arrays["in_consts"] = table
    consts = nc.dram_tensor("in_consts", table.shape, F32, kind="ExternalInput").ap()
    arrays["in_dists"] = distances()
    dists = nc.dram_tensor("in_dists", (P, 6 * P), F32, kind="ExternalInput").ap()
    outs = [nc.dram_tensor(f"out_{i}", shape, F32, kind="ExternalOutput").ap() for i, shape in enumerate(_OUTS)]
    trunk_kernel(nc, args, outs, consts, dists)
    r = run_bass_kernel_spmd(nc, [arrays], core_ids=[0])
    return tuple(r.results[0][f"out_{i}"] for i in range(len(_OUTS)))
```
